# Optimizing a Trainium2 kernel written in Bass

```python
import jax, jax.numpy as jnp
from jax import lax
import numpy as np

D_MODEL = 1024
BATCH = 1
SEQ = 512
DEPTH = 2
DEC_BATCH = 8
DEC_SEQ = 4
PAST_LEN = 1024
PAGE_SIZE = 128

N_META = 16
MLA_HEADS = 16
Q_LORA = 256
KV_LORA = 256
QK_NOPE = 64
QK_ROPE = 32
V_HEAD = 64
MLA_SCALE = (QK_NOPE + QK_ROPE) ** -0.5
ROPE_BASE = 10000.0
Q_BLOCK = 128
GLA_HEADS = 4
GLA_DK = D_MODEL // 2 // GLA_HEADS
GLA_DV = D_MODEL // GLA_HEADS
GLA_SCALE = GLA_DK ** -0.5
GATE_RANK = 16
GATE_TAU = 16.0
CHUNK = 64
D_FF = 4 * D_MODEL
EPS = 1e-6
N_MLA_LAYERS = (DEPTH + 1) // 2
N_GLA_LAYERS = DEPTH // 2

kernel_name = 'hybrid_mla_gla_decoder_step'

def rmsnorm(x, w):
    xf = x.astype(jnp.float32)
    y = xf * lax.rsqrt(jnp.mean(xf * xf, axis=-1, keepdims=True) + EPS)
    return (y * w.astype(jnp.float32)).astype(x.dtype)

def rope(x, pos):
    half = QK_ROPE // 2
    inv = ROPE_BASE ** (-jnp.arange(half, dtype=jnp.float32) / half)
    ang = pos.astype(jnp.float32)[:, None] * inv[None, :]
    ang = ang.reshape((ang.shape[0],) + (1,) * (x.ndim - 3) + (half,))
    cos, sin = jnp.cos(ang), jnp.sin(ang)
    x1, x2 = jnp.split(x.astype(jnp.float32), 2, axis=-1)
    return jnp.concatenate([x1 * cos - x2 * sin, x1 * sin + x2 * cos], axis=-1).astype(x.dtype)

def sq_relu_mlp(h, w_up, w_down):
    return jnp.square(jax.nn.relu(h @ w_up)) @ w_down

def mla_project(h, pos, w_in, q_norm, w_uq, kv_norm, w_uk):
    B, T, _ = h.shape
    a = h @ w_in
    cq, ckv, kpe = jnp.split(a, [Q_LORA, Q_LORA + KV_LORA], axis=-1)
    q = (rmsnorm(cq, q_norm) @ w_uq).reshape(B, T, MLA_HEADS, QK_NOPE + QK_ROPE)
    q_nope, q_pe = q[..., :QK_NOPE], q[..., QK_NOPE:]
    q_lat = jnp.einsum('bthn,chn->bthc', q_nope, w_uk)
    return q_lat, rope(q_pe, pos), rmsnorm(ckv, kv_norm), rope(kpe, pos)

def mla_scores(q_lat, q_pe, ckv, kpe):
    s = jnp.einsum('bqhc,bkc->bhqk', q_lat, ckv) + jnp.einsum('bqhr,bkr->bhqk', q_pe, kpe)
    return s.astype(jnp.float32) * MLA_SCALE

def mla_out(o_lat, w_uv, w_o):
    B, T = o_lat.shape[:2]
    o = jnp.einsum('bthc,chv->bthv', o_lat, w_uv).reshape(B, T, MLA_HEADS * V_HEAD)
    return o @ w_o

def mla_prompt(h, pos, w_in, q_norm, w_uq, kv_norm, w_uk, w_uv, w_o):
    q_lat, q_pe, ckv, kpe = mla_project(h, pos, w_in, q_norm, w_uq, kv_norm, w_uk)
    B, T = h.shape[:2]
    nqb = -(-T // Q_BLOCK)
    tq = nqb * Q_BLOCK

    def blocks(a):
        a = jnp.pad(a, ((0, 0), (0, tq - T)) + ((0, 0),) * (a.ndim - 2))
        return jnp.moveaxis(a.reshape((B, nqb, Q_BLOCK) + a.shape[2:]), 1, 0)

    qpos = jnp.arange(tq, dtype=jnp.int32).reshape(nqb, Q_BLOCK)
    kpos = jnp.arange(T, dtype=jnp.int32)

    def attend(args):
        ql, qp, qpos_b = args
        s = mla_scores(ql, qp, ckv, kpe)
        s = jnp.where(kpos[None, :] <= qpos_b[:, None], s, -jnp.inf)
        p = jax.nn.softmax(s, axis=-1).astype(ckv.dtype)
        return jnp.einsum('bhqk,bkc->bqhc', p, ckv)

    o_lat = lax.map(attend, (blocks(q_lat), blocks(q_pe), qpos))
    o_lat = jnp.moveaxis(o_lat, 0, 1).reshape(B, tq, MLA_HEADS, KV_LORA)[:, :T]
    return mla_out(o_lat, w_uv, w_o), ckv, kpe

def mla_sample(h, pos, cache_ckv, cache_kpe, layer, page_table, w_in, q_norm, w_uq, kv_norm, w_uk, w_uv, w_o):
    q_lat, q_pe, ckv_new, kpe_new = mla_project(h, pos, w_in, q_norm, w_uq, kv_norm, w_uk)
    DB, S = h.shape[:2]
    ckv_past = cache_ckv[layer, page_table].reshape(DB, -1, KV_LORA)
    kpe_past = cache_kpe[layer, page_table].reshape(DB, -1, QK_ROPE)
    P = ckv_past.shape[1]
    s_past = mla_scores(q_lat, q_pe, ckv_past, kpe_past)
    s_new = mla_scores(q_lat, q_pe, ckv_new, kpe_new)
    s_new = jnp.where(jnp.tril(jnp.ones((S, S), dtype=bool)), s_new, -jnp.inf)
    p = jax.nn.softmax(jnp.concatenate([s_past, s_new], axis=-1), axis=-1).astype(h.dtype)
    o_lat = (jnp.einsum('bhqk,bkc->bqhc', p[..., :P], ckv_past)
             + jnp.einsum('bhqk,bkc->bqhc', p[..., P:], ckv_new))
    return mla_out(o_lat, w_uv, w_o), ckv_new, kpe_new

def gla_recurrence(q, k, v, log_a, s0, lead):
    B, T, H, _ = q.shape
    total = lead + T
    nc = -(-total // CHUNK)
    pad = ((0, 0), (lead, nc * CHUNK - total), (0, 0), (0, 0))

    def chunks(t):
        t = jnp.pad(t.astype(jnp.float32), pad)
        return t.reshape(B, nc, CHUNK, H, t.shape[-1]).transpose(1, 0, 3, 2, 4)

    qc, kc, vc, gc = chunks(q), chunks(k), chunks(v), chunks(log_a)
    b = jnp.cumsum(gc, axis=3)
    b_last = b[:, :, :, -1:, :]
    q_in = qc * jnp.exp(b)
    k_in = kc * jnp.exp(-b)
    k_dec = kc * jnp.exp(b_last - b)
    causal = jnp.tril(jnp.ones((CHUNK, CHUNK), dtype=bool))
    A = jnp.where(causal, jnp.einsum('nbhid,nbhjd->nbhij', q_in, k_in), 0.0)
    o_intra = jnp.einsum('nbhij,nbhjv->nbhiv', A, vc)

    def step(s, xs):
        q_in_c, k_dec_c, v_c, bl = xs
        o_inter = jnp.einsum('bhid,bhdv->bhiv', q_in_c, s)
        s = jnp.exp(bl)[..., 0, :, None] * s + jnp.einsum('bhjd,bhjv->bhdv', k_dec_c, v_c)
        return s, o_inter

    s_fin, o_inter = lax.scan(step, s0.astype(jnp.float32), (q_in, k_dec, vc, b_last))
    o = (o_intra + o_inter).transpose(1, 0, 3, 2, 4).reshape(B, nc * CHUNK, H, -1)[:, lead:lead + T]
    return o, s_fin

def gla_mixer(h, s0, lead, w_in, w_gate, b_gate, g_norm, w_o):
    B, T, _ = h.shape
    hk = GLA_HEADS * GLA_DK
    hv = GLA_HEADS * GLA_DV
    a = h @ w_in
    q, k, v, r, gd = jnp.split(a, [hk, 2 * hk, 2 * hk + hv, 2 * hk + 2 * hv], axis=-1)

    def heads(t):
        return t.reshape(B, T, GLA_HEADS, -1)

    log_a = jax.nn.log_sigmoid((gd @ w_gate + b_gate).astype(jnp.float32)) / GATE_TAU
    o, s = gla_recurrence(heads(q) * GLA_SCALE, heads(k), heads(v), heads(log_a), s0, lead)
    o = rmsnorm(o.astype(h.dtype), g_norm) * jax.nn.silu(heads(r))
    return o.reshape(B, T, hv) @ w_o, s.astype(h.dtype)

def setup_inputs(seed: int = 0) -> dict:
    key = jax.random.key(seed)
    ks = jax.random.split(key, 32)
    f32 = jnp.float32

    def nrm(k, shape, scale=1.0):
        return jax.random.normal(k, shape, f32) * scale

    def gain(k, shape):
        return 1.0 + 0.01 * jax.random.normal(k, shape, f32)

    n_pages = PAST_LEN // PAGE_SIZE
    n_used = DEC_BATCH * n_pages
    n_pool = (n_used * 5) // 4
    page_table = jax.random.permutation(ks[5], n_pool)[:n_used].reshape(DEC_BATCH, n_pages).astype(jnp.int32)
    hk = GLA_HEADS * GLA_DK
    hv = GLA_HEADS * GLA_DV
    return {
        'x_prompt': nrm(ks[0], (BATCH, SEQ, D_MODEL)),
        'x_sample': nrm(ks[1], (DEC_BATCH, DEC_SEQ, D_MODEL)),
        'cache_ckv': nrm(ks[2], (N_MLA_LAYERS, n_pool, PAGE_SIZE, KV_LORA)),
        'cache_kpe': nrm(ks[3], (N_MLA_LAYERS, n_pool, PAGE_SIZE, QK_ROPE)),
        'state_gla': nrm(ks[4], (N_GLA_LAYERS, DEC_BATCH, GLA_HEADS, GLA_DK, GLA_DV), 0.5),
        'page_table': page_table,
        'meta_tokens': nrm(ks[6], (N_META, D_MODEL)),
        'norm_pre_mix': gain(ks[7], (DEPTH, D_MODEL)),
        'norm_post_mix': gain(ks[8], (DEPTH, D_MODEL)),
        'norm_pre_mlp': gain(ks[9], (DEPTH, D_MODEL)),
        'norm_post_mlp': gain(ks[10], (DEPTH, D_MODEL)),
        'mla_w_in': nrm(ks[11], (N_MLA_LAYERS, D_MODEL, Q_LORA + KV_LORA + QK_ROPE), D_MODEL ** -0.5),
        'mla_q_norm': gain(ks[12], (N_MLA_LAYERS, Q_LORA)),
        'mla_w_uq': nrm(ks[13], (N_MLA_LAYERS, Q_LORA, MLA_HEADS * (QK_NOPE + QK_ROPE)), Q_LORA ** -0.5),
        'mla_kv_norm': gain(ks[14], (N_MLA_LAYERS, KV_LORA)),
        'mla_w_uk': nrm(ks[15], (N_MLA_LAYERS, KV_LORA, MLA_HEADS, QK_NOPE), KV_LORA ** -0.5),
        'mla_w_uv': nrm(ks[16], (N_MLA_LAYERS, KV_LORA, MLA_HEADS, V_HEAD), KV_LORA ** -0.5),
        'mla_w_o': nrm(ks[17], (N_MLA_LAYERS, MLA_HEADS * V_HEAD, D_MODEL), (MLA_HEADS * V_HEAD) ** -0.5),
        'gla_w_in': nrm(ks[18], (N_GLA_LAYERS, D_MODEL, 2 * hk + 2 * hv + GATE_RANK), D_MODEL ** -0.5),
        'gla_w_gate': nrm(ks[19], (N_GLA_LAYERS, GATE_RANK, hk), GATE_RANK ** -0.5),
        'gla_b_gate': nrm(ks[20], (N_GLA_LAYERS, hk), 0.1),
        'gla_norm': gain(ks[21], (N_GLA_LAYERS, GLA_DV)),
        'gla_w_o': nrm(ks[22], (N_GLA_LAYERS, hv, D_MODEL), hv ** -0.5),
        'mlp_w_up': nrm(ks[23], (DEPTH, D_MODEL, D_FF), D_MODEL ** -0.5),
        'mlp_w_down': nrm(ks[24], (DEPTH, D_FF, D_MODEL), D_FF ** -0.5),
    }

def reference(x_prompt, x_sample, cache_ckv, cache_kpe, state_gla, page_table, meta_tokens,
              norm_pre_mix, norm_post_mix, norm_pre_mlp, norm_post_mlp,
              mla_w_in, mla_q_norm, mla_w_uq, mla_kv_norm, mla_w_uk, mla_w_uv, mla_w_o,
              gla_w_in, gla_w_gate, gla_b_gate, gla_norm, gla_w_o,
              mlp_w_up, mlp_w_down):
    B = x_prompt.shape[0]
    meta = jnp.broadcast_to(meta_tokens[None].astype(x_prompt.dtype), (B, N_META, D_MODEL))
    xp = jnp.concatenate([meta, x_prompt], axis=1)
    xs = x_sample
    past_len = page_table.shape[1] * cache_ckv.shape[2]
    pos_p = jnp.arange(xp.shape[1], dtype=jnp.int32)
    pos_s = past_len + jnp.arange(xs.shape[1], dtype=jnp.int32)

    ckv_p_l, kpe_p_l, ckv_s_l, kpe_s_l, gla_p_l, gla_s_l = [], [], [], [], [], []
    for i in range(DEPTH):
        j = i // 2
        hp = rmsnorm(xp, norm_pre_mix[i])
        hs = rmsnorm(xs, norm_pre_mix[i])
        if i % 2 == 0:
            w = (mla_w_in[j], mla_q_norm[j], mla_w_uq[j], mla_kv_norm[j], mla_w_uk[j], mla_w_uv[j], mla_w_o[j])
            mp, ckv_p, kpe_p = mla_prompt(hp, pos_p, *w)
            ms, ckv_s, kpe_s = mla_sample(hs, pos_s, cache_ckv, cache_kpe, j, page_table, *w)
            ckv_p_l.append(ckv_p)
            kpe_p_l.append(kpe_p)
            ckv_s_l.append(ckv_s)
            kpe_s_l.append(kpe_s)
        else:
            w = (gla_w_in[j], gla_w_gate[j], gla_b_gate[j], gla_norm[j], gla_w_o[j])
            s0 = jnp.zeros((B, GLA_HEADS, GLA_DK, GLA_DV), dtype=jnp.float32)
            mp, sp = gla_mixer(hp, s0, CHUNK - N_META, *w)
            ms, ss = gla_mixer(hs, state_gla[j], 0, *w)
            gla_p_l.append(sp)
            gla_s_l.append(ss)
        xp = xp + rmsnorm(mp, norm_post_mix[i])
        xs = xs + rmsnorm(ms, norm_post_mix[i])
        xp = xp + rmsnorm(sq_relu_mlp(rmsnorm(xp, norm_pre_mlp[i]), mlp_w_up[i], mlp_w_down[i]), norm_post_mlp[i])
        xs = xs + rmsnorm(sq_relu_mlp(rmsnorm(xs, norm_pre_mlp[i]), mlp_w_up[i], mlp_w_down[i]), norm_post_mlp[i])

    y_prompt = xp[:, N_META:]
    y_sample = xs
    new_ckv_prompt = jnp.stack(ckv_p_l)
    new_kpe_prompt = jnp.stack(kpe_p_l)
    new_ckv_sample = jnp.stack(ckv_s_l)
    new_kpe_sample = jnp.stack(kpe_s_l)
    new_gla_prompt = jnp.stack(gla_p_l)
    new_gla_sample = jnp.stack(gla_s_l)
    return (y_prompt, y_sample, new_ckv_prompt, new_kpe_prompt, new_ckv_sample, new_kpe_sample, new_gla_prompt, new_gla_sample)


_drawn_inputs = setup_inputs


def setup_inputs(seed=0):
    import zlib

    import numpy as np

    out = dict(_drawn_inputs(seed))
    spreads = {}
    factors = {'norm_pre_mix': 2.728,
     'norm_post_mix': 4.643,
     'norm_pre_mlp': 4.897,
     'norm_post_mlp': 5.555,
     'mla_q_norm': 5.424,
     'mla_kv_norm': 3.902,
     'gla_norm': 8.0}
    for name, (base, spread) in spreads.items():
        noise = np.random.default_rng([zlib.crc32(name.encode()), seed]).standard_normal(out[name].shape)
        drawn = base * np.exp(spread * noise) if base else spread * noise
        out[name] = __import__('jax').numpy.asarray(drawn.astype(out[name].dtype))
    for name, factor in factors.items():
        out[name] = (out[name] * factor).astype(out[name].dtype)
    return out
```

```python
from contextlib import ExitStack

import numpy as np
import concourse.bass as bass
from concourse import mybir

F32 = mybir.dt.float32
F32R = mybir.dt.float32r
I32 = mybir.dt.int32
ALU = mybir.AluOpType
ACT = mybir.ActivationFunctionType
AX_X = mybir.AxisListType.X

P = 128
D = 1024
DC = D // P
META, SEQ, NB, NS = 16, 512, 8, 4
NP = META + SEQ
NSAM = NB * NS
T = NP + NSAM
HALF = T // 2
FF = 4 * D
HEADS, NOPE, ROPE, VH = 16, 64, 32, 64
QH = NOPE + ROPE
LORA = 256
LC = LORA // P
PAGE = 128
PAGES = 8
PAST = PAGE * PAGES
SCALE = QH ** -0.5
GH, GK, GV = 4, 128, 256
GSCALE = GK ** -0.5
TAU = 16.0
RANK = 16
CH = 64
EPS = 1e-6
GLA_STEPS, GATE_STEPS = 9, 5

TILES = [(0, META)] + [(META + P * i, P) for i in range(SEQ // P)] + [(NP, NSAM)]
NT = len(TILES) - 1

NCH = 1 + SEQ // CH
ATT_BANK = (4, 7)
OG0 = CH - META


def chunk_at(c):
    if c == 0:
        return 0, META, 0, 0
    return CH * ((c - 1) % 2), CH, META + CH * (c - 1), 1 + (c - 1) // 2


G_MLA_IN = 0
G_MLA_O = G_MLA_IN + 4
G_MLP = [G_MLA_O + 8, 0]
G_GLA_IN = G_MLP[0] + 64
G_GLA_O = G_GLA_IN + 24
G_MLP[1] = G_GLA_O + 8
G_END = G_MLP[1] + 64
RAW, SPLIT = 4, 2

R_PRE_MIX, R_POST_MIX, R_PRE_MLP, R_POST_MLP = 0, 16, 32, 48
R_Q, R_KV, R_GLA, R_BG = 64, 66, 68, 70
N_GAIN = 74

NORMS = [(8, D), (2, LORA), (2, LORA), (8, D), (8, D), (8, D), (8, D)] + [(2, GV)] * GH + [(8, D)] * 3
(N_PRE_MIX0, N_CQ, N_CKV, N_POST_MIX0, N_PRE_MLP0, N_POST_MLP0, N_PRE_MIX1, N_GLA, _, _, _,
 N_POST_MIX1, N_PRE_MLP1, N_POST_MLP1) = range(14)
SQ0 = [sum(c for c, _ in NORMS[:n]) for n in range(len(NORMS) + 1)]

C_ID = 0
C_ROT = C_ID + P
C_COS = C_ROT + QH
C_SIN = C_COS + T
C_TRI = C_SIN + T
C_SMASK = C_TRI + P
C_GTRI = C_SMASK + NB * NSAM
C_GSAM = C_GTRI + CH
C_GBM = C_GSAM + NSAM
C_SCAN = C_GBM + NB
N_CONST = C_SCAN + T


def att_slot(c):
    return 0 if c == 0 else 2 - c % 2


def constants():
    c = np.zeros((P, N_CONST), np.float32)
    c[:, C_ID:C_ID + P] = np.eye(P)
    h = ROPE // 2
    rot = np.zeros((ROPE, ROPE), np.float32)
    rot[h + np.arange(h), np.arange(h)] = -1.0
    rot[np.arange(h), h + np.arange(h)] = 1.0
    pos = np.concatenate([np.arange(NP), np.tile(PAST + np.arange(NS), NB)]).astype(np.float32)
    inv = (np.float32(10000.0) ** (-np.arange(h, dtype=np.float32) / np.float32(h))).astype(np.float32)
    ang = (pos[None, :] * inv[:, None]).astype(np.float32)
    c[NOPE:QH, C_ROT + NOPE:C_ROT + QH] = rot
    c[NOPE:QH, C_COS:C_COS + T] = np.tile(np.cos(ang), (2, 1))
    c[NOPE:QH, C_SIN:C_SIN + T] = np.tile(np.sin(ang), (2, 1))
    i = np.arange(P)
    c[:, C_TRI:C_TRI + P] = np.where(i[None, :] <= i[:, None], 0.0, -1e30)
    s = np.arange(NSAM)
    for b in range(NB):
        ok = (s[None, :] // NS == b) & (s[None, :] % NS <= np.arange(HEADS * NS)[:, None] % NS)
        c[0:HEADS * NS, C_SMASK + b * NSAM:C_SMASK + (b + 1) * NSAM] = np.where(ok, 0.0, -1e30)
    j = np.arange(P) % CH
    c[:, C_GTRI:C_GTRI + CH] = np.where(j[:, None] <= np.arange(CH)[None, :], 1.0, 0.0)
    c[0:NSAM, C_GSAM:C_GSAM + NSAM] = np.where((s[:, None] // NS == s[None, :] // NS) & (s[:, None] <= s[None, :]), 1.0, 0.0)
    c[0:NSAM, C_GBM:C_GBM + NB] = np.where(s[:, None] // NS == np.arange(NB)[None, :], 1.0, 0.0)
    scan = np.ones(T, np.float32)
    scan[[0] + [META + CH * k for k in range(SEQ // CH)] + [NP + NS * b for b in range(NB)]] = 0.0
    c[:, C_SCAN:] = scan[None, :]
    return c


def trunk(nc, x_prompt, x_sample, cache_ckv, cache_kpe, state_gla, page_table, meta_tokens, norm_pre_mix,
          norm_post_mix, norm_pre_mlp, norm_post_mlp, mla_w_in, mla_q_norm, mla_w_uq, mla_kv_norm, mla_w_uk,
          mla_w_uv, mla_w_o, gla_w_in, gla_w_gate, gla_b_gate, gla_norm, gla_w_o, mlp_w_up, mlp_w_down, const,
          y_prompt, y_sample, new_ckv_prompt, new_kpe_prompt, new_ckv_sample, new_kpe_sample, new_gla_prompt,
          new_gla_sample):
    ctx = ExitStack()
    with ctx:
        def sb_in(scope, name, shape, dt=F32):
            return scope.enter_context(nc.sbuf_tensor(name, shape, dt))

        def sb(name, shape, dt=F32):
            return sb_in(ctx, name, shape, dt)

        def sem(name):
            return ctx.enter_context(nc.semaphore(name))

        cst = sb("cst", [P, N_CONST])
        gain = sb("gain", [P, N_GAIN])
        ones = sb("ones", [P, P])
        eps = sb("eps", [P, 1])
        x = sb("x", [P, DC, T])
        act_hi = sb("act_hi", [P, DC, T], F32R)
        act_lo = sb("act_lo", [P, DC, T], F32R)
        w_raw = [sb(f"w_raw{i}", [P, DC, P]) for i in range(RAW)]
        w_hi = [sb(f"w_hi{i}", [P, DC, P], F32R) for i in range(SPLIT)]
        w_lo = [sb(f"w_lo{i}", [P, DC, P], F32R) for i in range(SPLIT)]
        rstd_pre = sb("rstd_pre", [P, T])
        rstd_post = sb("rstd_post", [P, T])
        ssum = sb("ssum", [P, T])
        std = sb("std", [P, T])
        sq = [sb(f"sq{i}", [P, T]) for i in range(2)]

        with ExitStack() as s:
            x_tok = sb_in(s, "x_tok", [P, NT + 1, D])
            gain_rows = sb_in(s, "gain_rows", [N_GAIN, P])

        with ExitStack() as s:
            tail_raw = sb_in(s, "kpe_w_raw", [P, DC, ROPE])
            tail_hi = sb_in(s, "kpe_w_hi", [P, DC, ROPE], F32R)
            tail_lo = sb_in(s, "kpe_w_lo", [P, DC, ROPE], F32R)
            lat = sb_in(s, "lat", [P, 2 * LC, T])
            kT = sb_in(s, "kT", [QH, 2, T])
            uv = sb_in(s, "uv", [P, LC, HEADS * VH])
            qs = sb_in(s, "qs", [QH, HEADS, NSAM])
            ctok = sb_in(s, "ctok", [P, NT + 1, LORA + ROPE])
            pages = sb_in(s, "pages", [1, NB * PAGES], I32)
            with ExitStack() as s2:
                rope_tmp = sb_in(s2, "rope_tmp", [QH, T])
                v = sb_in(s2, "v", [P, NT, HEADS * VH])
                otok = sb_in(s2, "otok", [P, NT, HEADS * VH])
                qT = [sb_in(s2, f"qT{i}", [QH, T]) for i in range(2)]
                wq_pair = sb_in(s2, "wq_pair", [P, LC, 2 * QH])
                wk_pair = sb_in(s2, "wk_pair", [P, LC, 2 * NOPE])
                prob = [sb_in(s2, f"prob{i}", [P, NP]) for i in range(3)]
                probT = [sb_in(s2, f"probT{i}", [P, NT, P]) for i in range(2)]
                stat = sb_in(s2, "stat", [P, 3, 2 * NT])
            with ExitStack() as s2:
                qlat = sb_in(s2, "qlat", [P, LC, NB, HEADS * NS])
                qpe = sb_in(s2, "qpe", [ROPE, NB, HEADS * NS])
                kpe_new = sb_in(s2, "kpe_new", [ROPE, NSAM])
                olat = sb_in(s2, "olat", [P, LC, HEADS, NSAM])
                with ExitStack() as s3:
                    uk = sb_in(s3, "uk", [P, LC, HEADS * NOPE])
                    ukT = sb_in(s3, "ukT", [NOPE, HEADS, LORA])
                with ExitStack() as s3:
                    pg_ckv = [sb_in(s3, f"pg_ckv{i}", [P, PAGES, LORA]) for i in range(2)]
                    pg_kpe = [sb_in(s3, f"pg_kpe{i}", [P, PAGES, ROPE]) for i in range(2)]
                    ckT = sb_in(s3, "ckT", [P, LC, PAST])
                    kpT = sb_in(s3, "kpT", [ROPE, PAST])
                    qcur = [sb_in(s3, f"qcur{i}", [P, LC, HEADS * NS]) for i in range(2)]
                    qpcur = [sb_in(s3, f"qpcur{i}", [ROPE, HEADS * NS]) for i in range(2)]
                    sprob = sb_in(s3, "sprob", [P, PAST + NSAM])
                    sprobT = sb_in(s3, "sprobT", [P, PAGES, HEADS * NS])
                    sprobN = sb_in(s3, "sprobN", [NSAM, HEADS * NS])
                    sstat = sb_in(s3, "sstat", [HEADS * NS, 3])

        with ExitStack() as s:
            y = sb_in(s, "y", [P, DC, T])
            h_hi = sb_in(s, "h_hi", [P, DC, T], F32R)
            h_lo = sb_in(s, "h_lo", [P, DC, T], F32R)
            relu = [sb_in(s, f"relu{i}", [P, T]) for i in range(2)]
            relu2 = sb_in(s, "relu2", [P, T])
            out_tok = [sb_in(s, f"out_tok{i}", [P, D]) for i in range(2)]

        with ExitStack() as s:
            gqk = sb_in(s, "gqk", [P, 2 * GH, T])
            gr = sb_in(s, "gr", [P, DC, T])
            gv = sb_in(s, "gv", [P, NT + 1, GH * GV])
            with ExitStack() as s2:
                vT = [sb_in(s2, f"vT{i}", [P, T]) for i in range(4)]
                gd_raw = sb_in(s2, "gd_raw", [P, DC, RANK])
                gd_hi = sb_in(s2, "gd_hi", [P, DC, RANK], F32R)
                gd_lo = sb_in(s2, "gd_lo", [P, DC, RANK], F32R)
            with ExitStack() as s2:
                gdT = sb_in(s2, "gdT", [RANK, T])
                wg = sb_in(s2, "wg", [RANK, GH * GK])
                bcum = sb_in(s2, "bcum", [P, T])
                tA = sb_in(s2, "tA", [P, T])
                tB = sb_in(s2, "tB", [P, T])
                tC = sb_in(s2, "tC", [P, T])
                kd_tok = sb_in(s2, "kd_tok", [P, NT + 1, GK])
                kd_b = sb_in(s2, "kd_b", [NSAM, NB, GK])
                attT = sb_in(s2, "attT", [P, 3, CH])
                attS = sb_in(s2, "attS", [NSAM, NSAM])
                stp = [sb_in(s2, f"stp{i}", [P, GV]) for i in range(2)]
                sts = [sb_in(s2, f"sts{i}", [P, GV]) for i in range(4)]
                og = sb_in(s2, "og", [P, 2, T])

        ps = ctx.enter_context(nc.psum_tensor("ps", [P, 8, 512], F32))
        psf = ps[:, :, :].rearrange("p b n -> p (b n)")

        def blk_ps(g):
            return ps[:, 2 * (g % 2):2 * (g % 2) + 2, 0:HALF]

        def halves(ap):
            return ap.rearrange("p (h n) -> p h n", h=2)

        def chunk(ap):
            return ap.rearrange("p (o n) -> p o n", o=1)

        NORM_PS = ps[:, 6:8, 0:HALF]
        ident = cst[:, C_ID:C_ID + P]

        const_in = sem("const_in")
        gain_in = sem("gain_in")
        x_in = [sem(f"x_in{i}") for i in range(3)]
        ones_set = sem("ones_set")
        gain_turned = sem("gain_turned")
        gain_placed = sem("gain_placed")
        x_turned = sem("x_turned")
        x_placed = sem("x_placed")
        w_loaded = [sem(f"w_loaded{i}") for i in range(RAW)]
        w_rounded = sem("w_rounded")
        w_split = sem("w_split")
        blk_mm = sem("blk_mm")
        blk_read = sem("blk_read")
        squared = sem("squared")
        sq_added = sem("sq_added")
        summed = sem("summed")
        rooted = sem("rooted")
        inverted = sem("inverted")
        act_rounded = sem("act_rounded")
        act_ready = sem("act_ready")
        y_normed = sem("y_normed")
        x_updated = sem("x_updated")
        y_zeroed = sem("y_zeroed")
        h_rounded = sem("h_rounded")
        relu_squared = sem("relu_squared")
        h_ready = sem("h_ready")
        tail_in = sem("tail_in")
        tail_rounded = sem("tail_rounded")
        tail_split = sem("tail_split")
        tail_mm = sem("tail_mm")
        tail_read = sem("tail_read")
        krot_mm = sem("krot_mm")
        kpe_step = sem("kpe_step")
        kpe_ready = sem("kpe_ready")
        k_zeroed = sem("k_zeroed")
        att_zeroed = sem("att_zeroed")
        att_cleared = sem("att_cleared")
        lat_ready = sem("lat_ready")
        uv_in = sem("uv_in")
        pages_in = sem("pages_in")
        c_turned = sem("c_turned")
        c_placed = sem("c_placed")
        v_mm = sem("v_mm")
        v_placed = sem("v_placed")
        wq_in = sem("wq_in")
        wk_in = sem("wk_in")
        proj_mm = sem("proj_mm")
        rot_mm = sem("rot_mm")
        k_placed = sem("k_placed")
        q_placed = sem("q_placed")
        rope_step = sem("rope_step")
        q_roped = sem("q_roped")
        qs_saved = sem("qs_saved")
        s_mm = sem("s_mm")
        bias_ready = sem("bias_ready")
        exp_done = sem("exp_done")
        p_turned = sem("p_turned")
        p_placed = sem("p_placed")
        p_first = sem("p_first")
        rsum_inv = sem("rsum_inv")
        o_mm = sem("o_mm")
        o_placed = sem("o_placed")
        o_turned = sem("o_turned")
        o_rounded = sem("o_rounded")
        o_split = sem("o_split")
        uk_in = sem("uk_in")
        uk_turned = sem("uk_turned")
        uk_placed = sem("uk_placed")
        qlat_mm = sem("qlat_mm")
        qlat_ready = sem("qlat_ready")
        page_in = [sem(f"page_in{i}") for i in range(2)]
        pg_turned = sem("pg_turned")
        pg_placed = sem("pg_placed")
        qcur_ready = sem("qcur_ready")
        ss_mm = sem("ss_mm")
        ss_step = sem("ss_step")
        ss_bias = sem("ss_bias")
        ss_exp = sem("ss_exp")
        ss_norm = sem("ss_norm")
        sp_turned = sem("sp_turned")
        sp_placed = sem("sp_placed")
        so_mm = sem("so_mm")
        so_placed = sem("so_placed")
        gd_in = sem("gd_in")
        v_turned = sem("v_turned")
        gv_placed = sem("gv_placed")
        gate_step = sem("gate_step")
        gate_act = sem("gate_act")
        gate_mm = sem("gate_mm")
        gdT_ready = sem("gdT_ready")
        wg_in = sem("wg_in")
        gla_step = sem("gla_step")
        gla_act = sem("gla_act")
        qk_ready = sem("qk_ready")
        kd_turned = sem("kd_turned")
        kd_placed = sem("kd_placed")
        kdb_ready = sem("kdb_ready")
        att_mm = sem("att_mm")
        att_ready = sem("att_ready")
        up_mm = sem("up_mm")
        state_ready = sem("state_ready")
        og_mm = sem("og_mm")
        og_placed = sem("og_placed")
        satt_mm = sem("satt_mm")
        satt_ready = sem("satt_ready")
        st_in = [sem(f"st_in{i}") for i in range(4)]
        sup_mm = sem("sup_mm")
        st_ready = sem("st_ready")
        st_out = [sem(f"st_out{i}") for i in range(4)]
        gp_out = sem("gp_out")
        y_turned = sem("y_turned")
        y_placed = sem("y_placed")
        y_out = [sem(f"y_out{i}") for i in range(2)]
        c_out = sem("c_out")

        uq_v = mla_w_uq[0].rearrange("(c p) n -> p c n", p=P)
        uk_v = mla_w_uk[0].rearrange("(c p) h n -> p c (h n)", p=P)
        uv_v = mla_w_uv[0].rearrange("(c p) h n -> p c (h n)", p=P)

        def cols(w, at):
            return w.rearrange("(c p) m -> p c m", p=P)[:, :, bass.ds(at, P)]

        def raw_slot(g):
            return g % RAW

        block = ctx.enter_context(nc.Block())

        @block.sync
        def _(sp):
            def load_block(src, g, it=0):
                if g >= RAW:
                    sp.wait_ge(w_split, it * 4 + g - RAW + 1)
                sp.dma_start(w_raw[raw_slot(g)][:], src).then_inc(w_loaded[raw_slot(g)], 16)

            sp.dma_start(x_tok[0:META, 0, :], meta_tokens).then_inc(x_in[0], 16)
            sp.dma_start(x_tok[:, 1:NT, :], x_prompt[0].rearrange("(i p) d -> p i d", p=P)).then_inc(x_in[1], 16)
            sp.dma_start(x_tok[0:NSAM, NT, :], x_sample.rearrange("b s d -> (b s) d")).then_inc(x_in[2], 16)
            for g in range(4):
                load_block(cols(mla_w_in[0], g * P), G_MLA_IN + g)
            for j in range(4):
                load_block(cols(mla_w_o[0], j * P), G_MLA_O + j)
            sp.wait_ge(pages_in, 16)
            sp.wait_ge(qlat_mm, 1)
            with sp.Fori(0, NB // 2) as i:
                for s in range(2):
                    sp.wait_ge(so_mm, i * 2 + s - 2 + 1 + 2)
                    for g in range(PAGES):
                        n = sp.value_load(pages[0:1, bass.ds(i * (2 * PAGES) + s * PAGES + g, 1)], min_val=0,
                                          max_val=cache_ckv.shape[1] - 1)
                        sp.dma_start(pg_ckv[s][:, g, :], cache_ckv[0][bass.ds(n, 1)].rearrange("a p c -> p (a c)"))\
                            .then_inc(page_in[s], 16)
                        sp.dma_start(pg_kpe[s][:, g, :], cache_kpe[0][bass.ds(n, 1)].rearrange("a p c -> p (a c)"))\
                            .then_inc(page_in[s], 16)
            for j in range(4, 8):
                load_block(cols(mla_w_o[0], j * P), G_MLA_O + j)

            def mlp(layer):
                with sp.Fori(0, 4) as q:
                    with sp.Fori(0, 2) as it:
                        for j in range(4):
                            load_block(cols(mlp_w_up[layer], q * D + it * (4 * P) + j * P),
                                       G_MLP[layer] + j, q * 4 + it)
                    with sp.Fori(0, 2) as it:
                        for j in range(4):
                            load_block(cols(mlp_w_down[layer][bass.ds(q * D, D), :], it * (4 * P) + j * P),
                                       G_MLP[layer] + 8 + j, q * 4 + it)

            mlp(0)
            with sp.Fori(0, 6) as it:
                for j in range(4):
                    load_block(cols(gla_w_in[0], it * (4 * P) + j * P), G_GLA_IN + j, it)
            with sp.Fori(0, 2) as it:
                for j in range(4):
                    load_block(cols(gla_w_o[0], it * (4 * P) + j * P), G_GLA_O + j, it)
            mlp(1)
            for i, (t0, n) in enumerate(TILES[1:]):
                sp.wait_ge(y_placed, i + 1)
                dst = y_prompt[0, t0 - META:t0 - META + n, :] if i < NT - 1 else y_sample.rearrange("b s d -> (b s) d")
                sp.dma_start(dst, out_tok[i % 2][0:n, :]).then_inc(y_out[i % 2], 16)
            sp.wait_ge(y_out[0], 16 * 3)
            sp.wait_ge(y_out[1], 16 * 2)

        @block.gpsimd
        def _(pool):
            pool.dma_start(cst[:], const).then_inc(const_in, 16)
            for r, w in ((R_PRE_MIX, norm_pre_mix), (R_POST_MIX, norm_post_mix), (R_PRE_MLP, norm_pre_mlp),
                         (R_POST_MLP, norm_post_mlp)):
                pool.dma_start(gain_rows[r:r + 16, :], w.rearrange("l (c p) -> (l c) p", p=P)).then_inc(gain_in, 16)
            for r, w in ((R_Q, mla_q_norm), (R_KV, mla_kv_norm), (R_GLA, gla_norm), (R_BG, gla_b_gate)):
                k = w.shape[1] // P
                pool.dma_start(gain_rows[r:r + k, :], w.rearrange("l (c p) -> (l c) p", p=P)).then_inc(gain_in, 16)
            pool.dma_start(pages[:], page_table.rearrange("(o b) n -> o (b n)", o=1)).then_inc(pages_in, 16)
            nc.gpsimd.memset(ones[:], 1.0)
            nc.gpsimd.memset(eps[:], EPS).then_inc(ones_set, 1)
            pool.sem_inc(h_ready, 2)
            pool.sem_inc(qs_saved, 2)

            def add_square(n, c):
                k = SQ0[n] + c
                pool.wait_ge(squared, k + 1)
                if c == 0:
                    if n:
                        pool.wait_ge(summed, n)
                    nc.gpsimd.tensor_copy(ssum[:], sq[k % 2][:]).then_inc(sq_added, 1)
                else:
                    pool.wait_ge(sq_added, k)
                    nc.gpsimd.tensor_tensor(ssum[:], ssum[:], sq[k % 2][:], ALU.add).then_inc(sq_added, 1)

            def add_squares(n):
                for c in range(NORMS[n][0]):
                    add_square(n, c)

            def boundary(n_out, u, n_in=None):
                add_squares(n_out)
                for c in range(DC):
                    pool.wait_ge(y_normed, 8 * u + c + 1)
                    nc.gpsimd.tensor_tensor(x[:, c, :], x[:, c, :], y[:, c, :], ALU.add).then_inc(x_updated, 1)
                    if c and n_in is not None:
                        add_square(n_in, c - 1)
                if n_in is not None:
                    add_square(n_in, DC - 1)

            def mlp(layer):
                with pool.Fori(0, 4) as q:
                    with pool.Fori(0, 2) as it:
                        for j in range(4):
                            g = G_MLP[layer] + j + q * 16 + it * 4
                            n = layer * 32 + j + q * 8 + it * 4
                            pool.wait_ge(blk_read, g + 1)
                            pool.wait_ge(h_ready, n + 2)
                            nc.gpsimd.tensor_tensor(relu2[:], relu[j % 2][:], relu[j % 2][:], ALU.mult)\
                                .then_inc(relu_squared, 1)
                            pool.wait_ge(relu_squared, n + 1)
                            pool.wait_ge(h_rounded, n + 1)
                            nc.gpsimd.tensor_tensor(h_lo[:, bass.ds(it * 4 + j, 1), :], chunk(relu2[:]),
                                                    h_hi[:, bass.ds(it * 4 + j, 1), :].bitcast(F32), ALU.subtract)\
                                .then_inc(h_ready, 1)

            add_squares(N_PRE_MIX0)
            pool.wait_ge(x_placed, NT + 1)
            pool.wait_ge(gain_placed, 1)
            pool.dma_start(tail_raw[:], mla_w_in[0].rearrange("(c p) m -> p c m", p=P)[:, :, 2 * LORA:])\
                .then_inc(tail_in, 16)
            pool.dma_start(uv[:], uv_v).then_inc(uv_in, 16)
            nc.gpsimd.memset(kT[0:NOPE, 0, :], 0.0).then_inc(k_zeroed, 1)
            for t in prob:
                nc.gpsimd.memset(t[:], 0.0)
            for t in probT:
                nc.gpsimd.memset(t[:], 0.0)
            nc.gpsimd.memset(v[:, 0, :], 0.0).then_inc(att_zeroed, 1)
            add_squares(N_CQ)
            add_squares(N_CKV)
            for i, (t0, n) in enumerate(TILES):
                pool.wait_ge(c_placed, i + 1)
                if i < NT:
                    pool.dma_start(new_ckv_prompt[0, 0, t0:t0 + n, :], ctok[0:n, i, 0:LORA]).then_inc(c_out, 16)
                    pool.dma_start(new_kpe_prompt[0, 0, t0:t0 + n, :], ctok[0:n, i, LORA:]).then_inc(c_out, 16)
                else:
                    pool.dma_start(new_ckv_sample[0].rearrange("b s c -> (b s) c"), ctok[0:n, i, 0:LORA]).then_inc(c_out, 16)
                    pool.dma_start(new_kpe_sample[0].rearrange("b s c -> (b s) c"), ctok[0:n, i, LORA:]).then_inc(c_out, 16)
            with pool.Fori(0, HEADS // 2) as p:
                pool.wait_ge(proj_mm, p * 3 + 1)
                pool.dma_start(wq_pair[:], uq_v[:, :, bass.ds(p * (2 * QH), 2 * QH)]).then_inc(wq_in, 16)
                pool.dma_start(wk_pair[:], uk_v[:, :, bass.ds(p * (2 * NOPE), 2 * NOPE)]).then_inc(wk_in, 16)
                for hh in range(2):
                    pool.wait_ge(q_roped, p * 2 + hh + 1)
                    nc.gpsimd.tensor_copy(qs[:, bass.ds(p * 2 + hh, 1), :], chunk(qT[hh][:, NP:T]))\
                        .then_inc(qs_saved, 1)
            pool.wait_ge(o_turned, NT)
            pool.dma_start(uk[:], uk_v).then_inc(uk_in, 16)
            pool.wait_ge(c_out, 16 * 2 * (NT + 1))
            boundary(N_POST_MIX0, 0, N_PRE_MLP0)
            nc.gpsimd.memset(y[:], 0.0).then_inc(y_zeroed, 1)
            mlp(0)
            boundary(N_POST_MLP0, 1, N_PRE_MIX1)
            pool.wait_ge(x_updated, 16)
            pool.dma_start(gd_raw[:], gla_w_in[0].rearrange("(c p) m -> p c m", p=P)[:, :, 3 * D:]).then_inc(gd_in, 16)
            pool.wait_ge(gdT_ready, 1)
            pool.dma_start(wg[:], gla_w_gate[0]).then_inc(wg_in, 16)
            for h in range(GH):
                for b in range(NB):
                    k = h * NB + b
                    if b >= 4 or h:
                        pool.wait_ge(st_out[k % 4], 16 * (k // 4))
                    pool.dma_start(sts[k % 4][:], state_gla[0, b, h]).then_inc(st_in[k % 4], 16)
                    if k >= 3:
                        m = k - 3
                        pool.wait_ge(st_ready, m + 1)
                        pool.dma_start(new_gla_sample[0, m % NB, m // NB], sts[m % 4][:]).then_inc(st_out[m % 4], 16)
                    if b == 0 and h:
                        pool.wait_ge(state_ready, 9 * h)
                        pool.dma_start(new_gla_prompt[0, 0, h - 1], stp[0][:]).then_inc(gp_out, 16)
                        add_squares(N_GLA + h - 1)
            for m in range(GH * NB - 3, GH * NB):
                pool.wait_ge(st_ready, m + 1)
                pool.dma_start(new_gla_sample[0, m % NB, m // NB], sts[m % 4][:]).then_inc(st_out[m % 4], 16)
            pool.wait_ge(state_ready, 9 * GH)
            pool.dma_start(new_gla_prompt[0, 0, GH - 1], stp[0][:]).then_inc(gp_out, 16)
            add_squares(N_GLA + GH - 1)
            for i in range(4):
                pool.wait_ge(st_out[i], 16 * GH * NB // 4)
            pool.wait_ge(gp_out, 16 * GH)
            boundary(N_POST_MIX1, 2, N_PRE_MLP1)
            nc.gpsimd.memset(y[:], 0.0).then_inc(y_zeroed, 1)
            mlp(1)
            boundary(N_POST_MLP1, 3)

        @block.scalar
        def _(act):
            def round_block(g, it=0):
                act.wait_ge(w_loaded[raw_slot(g)], it * 16 + 16 * (g // RAW + 1))
                if g >= SPLIT:
                    act.wait_ge(blk_mm, it * 4 + g - SPLIT + 1)
                nc.scalar.copy(w_hi[g % SPLIT][:], w_raw[raw_slot(g)][:]).then_inc(w_rounded, 1)

            def square(n, c, src):
                k = SQ0[n] + c
                if k >= 2:
                    act.wait_ge(sq_added, k - 1)
                nc.scalar.activation(sq[k % 2][:], src, ACT.Square).then_inc(squared, 1)

            def root(n):
                act.wait_ge(summed, n + 1)
                if n:
                    act.wait_ge(inverted, n)
                nc.scalar.activation(halves(std[:]), NORM_PS, ACT.Sqrt, bias=eps[:, 0:1], scale=1.0 / NORMS[n][1])\
                    .then_inc(rooted, 1)

            def round_x(c, row):
                nc.scalar.activation(act_hi[:, c, :], x[:, c, :], ACT.Identity, scale=gain[:, row + c:row + c + 1])\
                    .then_inc(act_rounded, 1)

            def norm_in(n, row, u):
                for c in range(DC):
                    act.wait_ge(x_updated, 8 * u + c + 1)
                    square(n, c, x[:, c, :])
                    round_x(c, row)
                root(n)

            def square_y(n, it, j, g):
                k = SQ0[n] + j
                act.wait_ge(blk_read, it * 4 + g + j + 1)
                act.wait_ge(sq_added, it * 4 + k - 1)
                nc.scalar.activation(chunk(sq[j % 2][:]), y[:, bass.ds(it * 4 + j, 1), :], ACT.Square).then_inc(squared, 1)

            act.sem_inc(exp_done, 2)
            act.sem_inc(p_placed, 1)
            act.sem_inc(ss_exp, 1)
            act.sem_inc(sp_placed, 1)
            act.wait_ge(gain_placed, 1)
            act.wait_ge(x_placed, NT + 1)
            for c in range(DC):
                square(N_PRE_MIX0, c, x[:, c, :])
                round_x(c, R_PRE_MIX)
            round_block(0)
            round_block(1)
            root(N_PRE_MIX0)
            for g in range(4):
                round_block(g + 2)
            act.wait_ge(tail_in, 16)
            nc.scalar.copy(tail_hi[:], tail_raw[:]).then_inc(tail_rounded, 1)
            for n, c0 in ((N_CQ, 0), (N_CKV, LC)):
                for c in range(LC):
                    act.wait_ge(blk_read, c0 + c + 1)
                    square(n, c, lat[:, c0 + c, :])
                root(n)
            for i, (t0, n) in enumerate(TILES):
                act.wait_ge(c_turned, i + 1)
                nc.scalar.copy(ctok[0:n, i, :], ps[0:n, 4 + i % 2, 0:LORA + ROPE]).then_inc(c_placed, 1)
            act.wait_ge(att_zeroed, 1)
            for i, (t0, n) in enumerate(TILES[:NT]):
                act.wait_ge(v_mm, i + 1)
                nc.scalar.copy(v[0:n, i, :].rearrange("p (a n) -> p a n", a=2),
                               ps[0:n, 2 * (i % 2):2 * (i % 2) + 2, :]).then_inc(v_placed, 1)
            NST = 2 * NT
            with act.Fori(0, HEADS // 2) as p:
                act.wait_ge(proj_mm, p * 3 + 2)
                for hh in range(2):
                    nc.scalar.copy(kT[0:NOPE, hh, 0:NP].rearrange("p (a n) -> p a n", a=2),
                                   ps[NOPE * hh:NOPE * hh + NOPE, 0:2, 0:NP // 2]).then_inc(k_placed, 1)
                for n in range(NST + 2):
                    if n < NST:
                        rows = TILES[n % NT][1]
                        w = META + P * (n % NT)
                        act.wait_ge(bias_ready, p * NST + n + 1)
                        if n >= 3:
                            act.wait_ge(p_turned, p * NST + n - 2 + 2)
                        at = 1024 * (n % 2) + 512 - META
                        nc.scalar.activation(prob[n % 3][0:rows, 0:w], psf[0:rows, at:at + w], ACT.Exp,
                                             bias=stat[0:rows, 0, n:n + 1],
                                             accum_out=stat[0:rows, 1, n:n + 1]).then_inc(exp_done, 1)
                    if n >= 2:
                        m = n - 2
                        rows, nk = TILES[m % NT][1], m % NT
                        act.wait_ge(p_turned, p * NST + m + 1 + 2)
                        act.wait_ge(o_mm, p * NST + m - 1 + 2)
                        first = nc.scalar.copy(probT[m % 2][0:META, 0, 0:rows], psf[0:META, 2048:2048 + rows])
                        if nk == 0:
                            first.then_inc(p_placed, 1)
                        else:
                            first.then_inc(p_first, 1)
                            nc.scalar.copy(probT[m % 2][:, 1:1 + nk, 0:rows],
                                           psf[:, 2048 + P:2048 + P * (nk + 1)].rearrange("p (k n) -> p k n", n=P)[:, :, 0:rows])\
                                .then_inc(p_placed, 1)
            for i, (t0, n) in enumerate(TILES[:NT]):
                act.wait_ge(o_turned, i + 1)
                nc.scalar.copy(act_hi[:, :, t0:t0 + n], psf[:, 1024 * (i % 2):1024 * (i % 2) + 8 * n].rearrange("p (c n) -> p c n", c=DC))\
                    .then_inc(o_rounded, 1)
            for k in range(4):
                act.wait_ge(uk_turned, k + 1)
                nc.scalar.copy(ukT[:, 4 * k:4 * k + 4, :], psf[0:NOPE, 1024 * (k % 2):1024 * (k % 2) + 1024]
                               .rearrange("p (h c) -> p h c", h=4)).then_inc(uk_placed, 1)

            def place_pages(b, s):
                for k in range(3):
                    act.wait_ge(pg_turned, b * 3 + k + 1)
                    if k == 0:
                        act.wait_ge(ss_mm, b + 1)
                    src = psf[:, 1024 * ((s + k) % 2):1024 * ((s + k) % 2) + 1024]
                    if k < 2:
                        nc.scalar.copy(ckT[:, k, :], src).then_inc(pg_placed, 1)
                    else:
                        nc.scalar.copy(kpT[:], src[0:ROPE, :]).then_inc(pg_placed, 1)

            def sample_probs(b, s, last=False):
                act.wait_ge(ss_bias, b + 1)
                act.wait_ge(sp_turned, b + 1)
                nc.scalar.activation(sprob[0:HEADS * NS, :], psf[0:HEADS * NS, 2048:2048 + PAST + NSAM], ACT.Exp,
                                     bias=sstat[:, 0:1], accum_out=sstat[:, 1:2]).then_inc(ss_exp, 1)
                if not last:
                    place_pages(b + 1, 1 - s)
                act.wait_ge(sp_turned, b + 1 + 1)
                act.wait_ge(so_mm, b + 2)
                nc.scalar.copy(sprobN[:], ps[0:NSAM, 6, P:P + HEADS * NS])
                nc.scalar.copy(sprobT[:], ps[:, 7, :].rearrange("p (k n) -> p k n", k=PAGES)).then_inc(sp_placed, 1)

            place_pages(0, 0)
            with act.Fori(0, NB // 2 - 1) as i:
                for s in range(2):
                    sample_probs(i * 2 + s, s)
            for s in range(2):
                sample_probs(NB - 2 + s, s, last=(s == 1))
            act.wait_ge(o_turned, NT + 1)
            nc.scalar.copy(act_hi[:, :, NP:T], ps[:, 0, 0:DC * NSAM].rearrange("p (c n) -> p c n", c=DC)).then_inc(o_rounded, 1)
            with act.Fori(0, 2) as it:
                for j in range(4):
                    round_block(G_MLA_O + j + 2, it)
                    square_y(N_POST_MIX0, it, j, G_MLA_O)

            def boundary(n_out, n_in, row, u):
                root(n_out)
                norm_in(n_in, row, u)

            def mlp_up(layer, q):
                g0 = G_MLP[layer]
                with act.Fori(0, 2) as it:
                    for j in range(4):
                        round_block(g0 + j + 2, q * 4 + it)
                        act.wait_ge(blk_read, g0 + j + 1 + q * 16 + it * 4)
                        nc.scalar.activation(h_hi[:, bass.ds(it * 4 + j, 1), :], chunk(relu[j % 2][:]),
                                             ACT.Square).then_inc(h_rounded, 1)

            def mlp_down(layer, q):
                with act.Fori(0, 2) as it:
                    for j in range(4):
                        round_block(G_MLP[layer] + 8 + j + 2, q * 4 + it)

            boundary(N_POST_MIX0, N_PRE_MLP0, R_PRE_MLP, 0)
            with act.Fori(0, 3) as q:
                mlp_up(0, q)
                mlp_down(0, q)
            mlp_up(0, 3)
            with act.Fori(0, 2) as it:
                for j in range(4):
                    round_block(G_MLP[0] + 56 + j + 2, it)
                    square_y(N_POST_MLP0, it, j, G_MLP[0] + 56)
            boundary(N_POST_MLP0, N_PRE_MIX1, R_PRE_MIX + 8, 1)
            with act.Fori(0, 6) as it:
                for j in range(4):
                    round_block(G_GLA_IN + j + 2, it)
            act.wait_ge(gd_in, 16)
            nc.scalar.copy(gd_hi[:], gd_raw[:]).then_inc(tail_rounded, 1)
            for h in range(GH):
                act.wait_ge(gate_mm, h + 1)
                if h:
                    act.wait_ge(kd_turned, h)
                    act.wait_ge(gate_step, GATE_STEPS * 2 * h)
                nc.scalar.activation(halves(tA[:]), ps[:, 4:6, 0:HALF], ACT.Abs,
                                     bias=gain[:, R_BG + h:R_BG + h + 1]).then_inc(gla_act, 1)
                act.wait_ge(gla_act, 6 * h + 1)
                nc.scalar.activation(tA[:], tA[:], ACT.Exp, scale=-1.0).then_inc(gla_act, 1)
                act.wait_ge(gla_act, 6 * h + 2)
                nc.scalar.activation(tA[:], tA[:], ACT.Ln, bias=1.0).then_inc(gla_act, 1)
                act.wait_ge(gla_step, GLA_STEPS * h + 3)
                nc.scalar.activation(tB[:], bcum[:], ACT.Exp, scale=1.0 / TAU).then_inc(gla_act, 1)
                nc.scalar.activation(tC[:], bcum[:], ACT.Exp, scale=-1.0 / TAU).then_inc(gla_act, 1)
                act.wait_ge(gla_step, GLA_STEPS * h + 7)
                nc.scalar.activation(tA[:], tA[:], ACT.Exp, scale=1.0 / TAU).then_inc(gla_act, 1)
                act.wait_ge(kd_turned, h + 1)
                if h:
                    act.wait_ge(sup_mm, NB * h)
                nc.scalar.copy(kd_tok[0:META, 0, :], psf[0:META, 2048:2048 + GK])
                nc.scalar.copy(kd_tok[:, 1:NT, :], psf[:, 2048 + GK:2048 + NT * GK].rearrange("p (i n) -> p i n", n=GK))
                nc.scalar.copy(kd_tok[0:NSAM, NT, :], psf[0:NSAM, 2048 + NT * GK:2048 + (NT + 1) * GK]).then_inc(kd_placed, 1)
                for c in range(2):
                    act.wait_ge(og_placed, 2 * h + c + 1)
                    square(N_GLA + h, c, og[:, c, :])
                root(N_GLA + h)
                for c in range(2):
                    k = 2 * h + c
                    if c:
                        act.wait_ge(gate_step, GATE_STEPS * k)
                    else:
                        act.wait_ge(gla_step, GLA_STEPS * h + 9)
                    nc.scalar.activation(tC[:], gr[:, k, :], ACT.Exp, scale=-1.0).then_inc(gate_act, 1)
                    act.wait_ge(gate_step, GATE_STEPS * k + 5)
                    nc.scalar.copy(act_hi[:, k, :], og[:, c, :]).then_inc(act_rounded, 1)
            with act.Fori(0, 2) as it:
                for j in range(4):
                    round_block(G_GLA_O + j + 2, it)
                    square_y(N_POST_MIX1, it, j, G_GLA_O)
            boundary(N_POST_MIX1, N_PRE_MLP1, R_PRE_MLP + 8, 2)
            with act.Fori(0, 3) as q:
                mlp_up(1, q)
                mlp_down(1, q)
            mlp_up(1, 3)
            for j in range(8):
                if j < 6:
                    round_block(G_MLP[1] + 56 + j + 2)
                square_y(N_POST_MLP1, j // 4, j % 4, G_MLP[1] + 56)
            root(N_POST_MLP1)

        @block.vector
        def _(dve):
            def split_block(g, it=0):
                dve.wait_ge(w_rounded, it * 4 + g + 1)
                nc.vector.tensor_tensor(w_lo[g % SPLIT][:], w_raw[raw_slot(g)][:], w_hi[g % SPLIT][:].bitcast(F32),
                                        ALU.subtract).then_inc(w_split, 1)

            def invert(n, out):
                dve.wait_ge(rooted, n + 1)
                nc.vector.reciprocal(out[:], std[:]).then_inc(inverted, 1)

            def split_x(f, c, row):
                dve.wait_ge(act_rounded, 8 * f + c + 1)
                nc.vector.scalar_tensor_tensor(act_lo[:, c, :], x[:, c, :], gain[:, row + c:row + c + 1],
                                               act_hi[:, c, :].bitcast(F32), ALU.mult, ALU.subtract).then_inc(act_ready, 1)

            def boundary(n_out, row_out, u, n_in, f, row_in):
                invert(n_out, rstd_post)
                dve.wait_ge(inverted, n_out + 1)
                for c in range(DC):
                    nc.vector.scalar_tensor_tensor(y[:, c, :], y[:, c, :], gain[:, row_out + c:row_out + c + 1],
                                                   rstd_post[:], ALU.mult, ALU.mult).then_inc(y_normed, 1)
                    if c >= 2 and n_in is not None:
                        split_x(f, c - 2, row_in)
                if n_in is not None:
                    for c in range(DC - 2, DC):
                        split_x(f, c, row_in)
                    invert(n_in, rstd_pre)
                    dve.wait_ge(inverted, n_in + 1)

            dve.wait_ge(gain_turned, 1)
            nc.vector.tensor_copy(gain[:], ps[:, 4, 0:N_GAIN]).then_inc(gain_placed, 1)
            dve.sem_inc(o_placed, 2)
            dve.sem_inc(so_placed, 1)
            for i, (t0, n) in enumerate(TILES):
                dve.wait_ge(x_turned, i + 1)
                nc.vector.tensor_copy(x[:, :, t0:t0 + n], psf[:, 1024 * (i % 2):1024 * (i % 2) + DC * n]
                                      .rearrange("p (c n) -> p c n", c=DC)).then_inc(x_placed, 1)
            dve.wait_ge(gain_placed, 1)
            dve.wait_ge(x_placed, NT + 1)
            for c in range(DC):
                split_x(0, c, R_PRE_MIX)
            split_block(0)
            split_block(1)
            invert(N_PRE_MIX0, rstd_pre)
            dve.wait_ge(inverted, N_PRE_MIX0 + 1)
            for g in range(4):
                dve.wait_ge(blk_mm, g + 1)
                nc.vector.tensor_tensor(halves(lat[:, g, :]), blk_ps(g), halves(rstd_pre[:]), ALU.mult).then_inc(blk_read, 1)
                split_block(g + 2)
            dve.wait_ge(tail_rounded, 1)
            nc.vector.tensor_tensor(tail_lo[:], tail_raw[:], tail_hi[:].bitcast(F32), ALU.subtract).then_inc(tail_split, 1)
            kr = kT[NOPE:QH, 0, :]
            dve.wait_ge(tail_mm, 1)
            nc.vector.tensor_tensor(halves(kr), ps[0:ROPE, 4:6, 0:HALF], halves(rstd_pre[0:ROPE, :]), ALU.mult).then_inc(tail_read, 1)
            cos, sin = cst[NOPE:QH, C_COS:C_COS + T], cst[NOPE:QH, C_SIN:C_SIN + T]
            dve.wait_ge(krot_mm, 1)
            nc.vector.tensor_tensor(halves(rope_tmp[NOPE:QH, :]), ps[NOPE:QH, 4:6, 0:HALF], halves(sin), ALU.mult).then_inc(kpe_step, 1)
            nc.vector.tensor_tensor(kr, kr, cos, ALU.mult).then_inc(kpe_step, 1)
            dve.wait_ge(kpe_step, 2)
            nc.vector.tensor_tensor(kr, kr, rope_tmp[NOPE:QH, :], ALU.add).then_inc(kpe_step, 1)
            dve.wait_ge(kpe_step, 3)
            nc.vector.tensor_copy(kT[NOPE:QH, 1, :], kr).then_inc(kpe_ready, 1)
            for n, row, c0 in ((N_CQ, R_Q, 0), (N_CKV, R_KV, LC)):
                invert(n, rstd_post)
                dve.wait_ge(inverted, n + 1)
                for c in range(LC):
                    nc.vector.scalar_tensor_tensor(lat[:, c0 + c, :], lat[:, c0 + c, :], gain[:, row + c:row + c + 1],
                                                   rstd_post[:], ALU.mult, ALU.mult).then_inc(lat_ready, 1)
                dve.wait_ge(lat_ready, c0 + LC)
            NST = 2 * NT
            with dve.Fori(0, HEADS // 2) as p:
                for hh in range(2):
                    dve.wait_ge(proj_mm, p * 3 + hh + 3)
                    dve.wait_ge(qs_saved, p * 2 + hh + 1)
                    nc.vector.tensor_scalar(halves(qT[hh][:]), ps[0:QH, 2 + 2 * hh:4 + 2 * hh, 0:HALF], SCALE, None, ALU.mult)\
                        .then_inc(q_placed, 1)
                for hh in range(2):
                    qr = qT[hh][NOPE:QH, :]
                    dve.wait_ge(rot_mm, p * 2 + hh + 1)
                    at = 6 if hh == 0 else 0
                    nc.vector.tensor_tensor(halves(rope_tmp[NOPE:QH, :]), ps[NOPE:QH, at:at + 2, 0:HALF], halves(sin), ALU.mult)\
                        .then_inc(rope_step, 1)
                    nc.vector.tensor_tensor(qr, qr, cos, ALU.mult).then_inc(rope_step, 1)
                    dve.wait_ge(rope_step, p * 4 + hh * 2 + 2)
                    nc.vector.tensor_tensor(qr, qr, rope_tmp[NOPE:QH, :], ALU.add).then_inc(q_roped, 1)
                    dve.wait_ge(q_roped, p * 2 + hh + 1)
                for n in range(NST + 3):
                    if n < NST:
                        rows = TILES[n % NT][1]
                        w = META + P * (n % NT)
                        at = 1024 * (n % 2) + 512 - META
                        dve.wait_ge(s_mm, p * NST + n + 1)
                        nc.vector.tensor_reduce(stat[0:rows, 0, n:n + 1], psf[0:rows, at:at + w], AX_X, ALU.max,
                                                negate=True).then_inc(bias_ready, 1)
                    if 1 <= n <= NST:
                        m = n - 1
                        rows = TILES[m % NT][1]
                        dve.wait_ge(exp_done, p * NST + m + 1 + 2)
                        nc.vector.reciprocal(stat[0:rows, 2, m:m + 1], stat[0:rows, 1, m:m + 1]).then_inc(rsum_inv, 1)
                    if n >= 3:
                        m = n - 3
                        rows = TILES[m % NT][1]
                        dve.wait_ge(o_mm, p * NST + m + 1 + 2)
                        dve.wait_ge(rsum_inv, p * NST + m + 1)
                        nc.vector.tensor_scalar(otok[0:rows, m % NT, bass.ds(p * (2 * VH) + (m // NT) * VH, VH)],
                                                ps[0:rows, 6 + m % 2, 0:VH], stat[0:rows, 2, m:m + 1], None, ALU.mult)\
                            .then_inc(o_placed, 1)
            for i, (t0, n) in enumerate(TILES[:NT]):
                dve.wait_ge(o_rounded, i + 1)
                nc.vector.tensor_tensor(act_lo[:, :, t0:t0 + n], psf[:, 1024 * (i % 2):1024 * (i % 2) + 8 * n]
                                        .rearrange("p (c n) -> p c n", c=DC), act_hi[:, :, t0:t0 + n].bitcast(F32),
                                        ALU.subtract).then_inc(o_split, 1)
            dve.wait_ge(qlat_mm, 1)
            for c in range(LC):
                nc.vector.tensor_copy(qlat[:, c, :, :].rearrange("p b (h s) -> p b h s", s=NS),
                                      ps[:, 4 + c, :].rearrange("p (h b s) -> p b h s", b=NB, s=NS)).then_inc(qlat_ready, 1)
            nc.vector.tensor_copy(qpe[:, :, :].rearrange("p b (h s) -> p b h s", s=NS),
                                  qs[NOPE:QH, :, :].rearrange("p h (b s) -> p b h s", s=NS)).then_inc(qlat_ready, 1)
            nc.vector.tensor_copy(kpe_new[:], kT[NOPE:QH, 0, NP:T]).then_inc(qlat_ready, 1)
            dve.wait_ge(qlat_ready, 4)

            def take_queries(b, s):
                nc.vector.tensor_copy(qcur[s][:].rearrange("p c (o n) -> p c o n", o=1),
                                      qlat[:, :, bass.ds(b, 1), :])
                nc.vector.tensor_copy(chunk(qpcur[s][:]), qpe[:, bass.ds(b, 1), :]).then_inc(qcur_ready, 1)

            def sample_stats(b, s, last=False):
                dve.wait_ge(ss_mm, b + 1 + 1)
                new = ps[0:HEADS * NS, 6, 0:NSAM]
                nc.vector.tensor_tensor(new, new, cst[0:HEADS * NS, bass.ds(b * NSAM + C_SMASK, NSAM)], ALU.add).then_inc(ss_step, 1)
                dve.wait_ge(ss_step, b * 2 + 1)
                nc.vector.tensor_reduce(sstat[:, 0:1], psf[0:HEADS * NS, 2048:2048 + PAST + NSAM], AX_X, ALU.max,
                                        negate=True).then_inc(ss_bias, 1)
                if not last:
                    take_queries(b + 1, 1 - s)
                dve.wait_ge(ss_exp, b + 1 + 1)
                nc.vector.reciprocal(sstat[:, 2:3], sstat[:, 1:2]).then_inc(ss_step, 1)
                dve.wait_ge(ss_step, b * 2 + 2)
                nc.vector.tensor_scalar(sprob[0:HEADS * NS, :], sprob[0:HEADS * NS, :], sstat[:, 2:3], None, ALU.mult).then_inc(ss_norm, 1)
                dve.wait_ge(so_mm, b + 1 + 2)
                nc.vector.tensor_copy(olat[:, :, :, bass.ds(b * NS, NS)],
                                      ps[:, 6, 256:256 + LC * HEADS * NS].rearrange("p (c h s) -> p c h s", c=LC, s=NS))\
                    .then_inc(so_placed, 1)

            nc.vector.memset(sprob[HEADS * NS:P, :], 0.0).then_inc(qcur_ready, 1)
            take_queries(0, 0)
            with dve.Fori(0, NB // 2 - 1) as i:
                for s in range(2):
                    sample_stats(i * 2 + s, s)
            for s in range(2):
                sample_stats(NB - 2 + s, s, last=(s == 1))
            dve.wait_ge(o_rounded, NT + 1)
            nc.vector.tensor_tensor(act_lo[:, :, NP:T], ps[:, 0, 0:DC * NSAM].rearrange("p (c n) -> p c n", c=DC),
                                    act_hi[:, :, NP:T].bitcast(F32), ALU.subtract).then_inc(o_split, 1)

            def product_to_y(g0):
                with dve.Fori(0, 2) as it:
                    for j in range(4):
                        dve.wait_ge(blk_mm, it * 4 + g0 + j + 1)
                        nc.vector.tensor_copy(y[:, bass.ds(it * 4 + j, 1), :].rearrange("p o (h n) -> p (o h) n", h=2),
                                              blk_ps(g0 + j)).then_inc(blk_read, 1)
                        split_block(g0 + j + 2, it)

            def mlp_up(layer, q):
                g0 = G_MLP[layer]
                with dve.Fori(0, 2) as it:
                    for j in range(4):
                        n = it * 4 + q * 8 + layer * 32 + j
                        dve.wait_ge(blk_mm, it * 4 + q * 16 + g0 + j + 1)
                        dve.wait_ge(h_ready, n + 1)
                        nc.vector.scalar_tensor_tensor(halves(relu[j % 2][:]), blk_ps(g0 + j), 0.0, halves(rstd_pre[:]),
                                                       ALU.max, ALU.mult).then_inc(blk_read, 1)
                        split_block(g0 + j + 2, q * 4 + it)

            def add_down(g, it, m, ahead=True):
                dve.wait_ge(blk_mm, it * 4 + g + 1)
                dve.wait_ge(blk_read, it * 4 + g)
                yc = y[:, bass.ds(m, 1), :].rearrange("p o (h n) -> p (o h) n", h=2)
                nc.vector.tensor_tensor(yc, blk_ps(g), yc, ALU.add).then_inc(blk_read, 1)
                if ahead:
                    split_block(g + 2, it)

            def mlp_down(layer, q):
                with dve.Fori(0, 2) as it:
                    for j in range(4):
                        add_down(G_MLP[layer] + 8 + j, q * 4 + it, it * 4 + j)

            dve.wait_ge(c_out, 16 * 2 * (NT + 1))
            product_to_y(G_MLA_O)
            boundary(N_POST_MIX0, R_POST_MIX, 0, N_PRE_MLP0, 1, R_PRE_MLP)
            dve.wait_ge(y_zeroed, 1)
            with dve.Fori(0, 4) as q:
                mlp_up(0, q)
                mlp_down(0, q)
            boundary(N_POST_MLP0, R_POST_MLP, 1, N_PRE_MIX1, 2, R_PRE_MIX + 8)
            with dve.Fori(0, 2) as it:
                for j in range(4):
                    dve.wait_ge(blk_mm, it * 4 + G_GLA_IN + j + 1)
                    nc.vector.tensor_tensor(gqk[:, bass.ds(it * 4 + j, 1), :].rearrange("p o (h n) -> p (o h) n", h=2),
                                            blk_ps(j), halves(rstd_pre[:]), ALU.mult).then_inc(blk_read, 1)
                    split_block(G_GLA_IN + j + 2, it)
            nc.vector.memset(gv[:, 0, :], 0.0).then_inc(att_cleared, 1)
            dve.wait_ge(att_cleared, 1)
            with dve.Fori(0, 2) as it:
                for j in range(4):
                    dve.wait_ge(blk_mm, it * 4 + G_GLA_IN + 8 + j + 1)
                    nc.vector.tensor_tensor(halves(vT[j][:]), blk_ps(j), halves(rstd_pre[:]), ALU.mult).then_inc(blk_read, 1)
                    split_block(G_GLA_IN + 8 + j + 2, it)
                for i, (t0, n) in enumerate(TILES):
                    dve.wait_ge(v_turned, it * (NT + 1) + i + 1)
                    nc.vector.tensor_copy(gv[0:n, i, bass.ds(it * 512, 512)], ps[0:n, 4 + i % 2, :]).then_inc(gv_placed, 1)
            with dve.Fori(0, 2) as it:
                for j in range(4):
                    dve.wait_ge(blk_mm, it * 4 + G_GLA_IN + 16 + j + 1)
                    nc.vector.tensor_tensor(gr[:, bass.ds(it * 4 + j, 1), :].rearrange("p o (h n) -> p (o h) n", h=2),
                                            blk_ps(j), halves(rstd_pre[:]), ALU.mult).then_inc(blk_read, 1)
                    split_block(G_GLA_IN + 16 + j + 2, it)
            dve.wait_ge(tail_rounded, 2)
            nc.vector.tensor_tensor(gd_lo[:], gd_raw[:], gd_hi[:].bitcast(F32), ALU.subtract).then_inc(tail_split, 1)
            dve.wait_ge(tail_mm, 2)
            nc.vector.tensor_tensor(halves(gdT[:]), ps[0:RANK, 4:6, 0:HALF], halves(rstd_pre[0:RANK, :]), ALU.mult)\
                .then_inc(gdT_ready, 1)
            step_count = 0
            nc.vector.memset(attT[:], 0.0).then_inc(att_cleared, 1)
            dve.wait_ge(att_cleared, 2)

            def step(ins):
                nonlocal step_count
                step_count += 1
                ins.then_inc(gla_step, 1)
                dve.wait_ge(gla_step, step_count)

            for h in range(GH):
                gq, gk = gqk[:, h, :], gqk[:, GH + h, :]
                dve.wait_ge(gla_act, 6 * h + 1)
                step(nc.vector.tensor_scalar(halves(tB[:]), ps[:, 4:6, 0:HALF], gain[:, R_BG + h:R_BG + h + 1], 0.0, ALU.add, ALU.min))
                dve.wait_ge(gla_act, 6 * h + 3)
                step(nc.vector.tensor_tensor(tB[:], tB[:], tA[:], ALU.subtract))
                step(nc.vector.tensor_tensor_scan(bcum[:], cst[:, C_SCAN:C_SCAN + T], tB[:], 0.0, ALU.mult, ALU.add))
                for t0, n, k in ((0, META, 1), (META, CH, SEQ // CH), (NP, NS, NB)):
                    if t0 == 0:
                        dve.wait_ge(gla_act, 6 * h + 4)
                        step(nc.vector.scalar_tensor_tensor(gq, gq, GSCALE, tB[:], ALU.mult, ALU.mult))
                    b3 = bcum[:, t0:t0 + n * k].rearrange("p (k n) -> p k n", n=n)
                    step(nc.vector.tensor_tensor(tA[:, t0:t0 + n * k].rearrange("p (k n) -> p k n", n=n),
                                                 b3[:, :, n - 1:n].to_broadcast([P, k, n]), b3, ALU.subtract))
                dve.wait_ge(gla_act, 6 * h + 6)
                step(nc.vector.tensor_tensor(tA[:], gk, tA[:], ALU.mult))
                step(nc.vector.tensor_tensor(gk, gk, tC[:], ALU.mult))
                dve.wait_ge(kd_placed, h + 1)
                nc.vector.tensor_tensor(kd_b[:], kd_tok[0:NSAM, NT:NT + 1, :].to_broadcast([NSAM, NB, GK]),
                                        chunk(cst[0:NSAM, C_GBM:C_GBM + NB]).rearrange("p o b -> p b o").to_broadcast([NSAM, NB, GK]),
                                        ALU.mult).then_inc(kdb_ready, 1)
                for c in range(NCH):
                    base, n, t0, _ = chunk_at(c)
                    k = h * NCH + c
                    dve.wait_ge(att_mm, k + 1)
                    if k >= 2:
                        dve.wait_ge(og_mm, k - 1)
                    nc.vector.tensor_tensor(attT[base:base + n, att_slot(c), 0:n], ps[base:base + n, ATT_BANK[c % 2], 0:n],
                                            cst[base:base + n, C_GTRI:C_GTRI + n], ALU.mult).then_inc(att_ready, 1)
                    dve.wait_ge(up_mm, k + 1)
                    up = ps[:, 5 + c % 2, 0:GV]
                    if c == 0:
                        if h:
                            dve.wait_ge(gp_out, 16 * h)
                        nc.vector.tensor_copy(stp[0][:], up).then_inc(state_ready, 1)
                    else:
                        dve.wait_ge(og_mm, k)
                        dve.wait_ge(state_ready, k)
                        nc.vector.scalar_tensor_tensor(stp[c % 2][:], stp[(c - 1) % 2][:], tB[:, t0 + n - 1:t0 + n], up,
                                                       ALU.mult, ALU.add).then_inc(state_ready, 1)
                dve.wait_ge(satt_mm, h + 1)
                nc.vector.tensor_tensor(attS[:], ps[0:NSAM, 4, P:P + NSAM], cst[0:NSAM, C_GSAM:C_GSAM + NSAM], ALU.mult)\
                    .then_inc(satt_ready, 1)
                for b in range(NB):
                    k = h * NB + b
                    dve.wait_ge(sup_mm, k + 1)
                    nc.vector.scalar_tensor_tensor(sts[k % 4][:], sts[k % 4][:], tB[:, NP + NS * b + NS - 1:NP + NS * b + NS],
                                                   ps[:, 5 + b % 2, 0:GV], ALU.mult, ALU.add)\
                        .then_inc(st_ready, 1)
                for c in range(2):
                    nc.vector.tensor_copy(og[:, c, :], psf[:, 1024 * c + OG0:1024 * c + OG0 + T]).then_inc(og_placed, 1)
                invert(N_GLA + h, rstd_post)
                for c in range(2):
                    k = 2 * h + c
                    dve.wait_ge(gate_act, k + 1)
                    nc.vector.tensor_scalar(tC[:], tC[:], 1.0, None, ALU.add).then_inc(gate_step, 1)
                    dve.wait_ge(gate_step, GATE_STEPS * k + 1)
                    nc.vector.reciprocal(tC[:], tC[:]).then_inc(gate_step, 1)
                    dve.wait_ge(gate_step, GATE_STEPS * k + 2)
                    nc.vector.tensor_tensor(tC[:], tC[:], gr[:, k, :], ALU.mult).then_inc(gate_step, 1)
                    dve.wait_ge(inverted, N_GLA + h + 1)
                    nc.vector.scalar_tensor_tensor(og[:, c, :], og[:, c, :], gain[:, R_GLA + c:R_GLA + c + 1], rstd_post[:],
                                                   ALU.mult, ALU.mult).then_inc(gate_step, 1)
                    dve.wait_ge(gate_step, GATE_STEPS * k + 4)
                    nc.vector.tensor_tensor(og[:, c, :], og[:, c, :], tC[:], ALU.mult).then_inc(gate_step, 1)
                    dve.wait_ge(act_rounded, 8 * 3 + k + 1)
                    dve.wait_ge(gate_step, GATE_STEPS * k + 5)
                    nc.vector.tensor_tensor(act_lo[:, k, :], og[:, c, :], act_hi[:, k, :].bitcast(F32), ALU.subtract)\
                        .then_inc(act_ready, 1)
            dve.wait_ge(gp_out, 16 * GH)
            for i in range(4):
                dve.wait_ge(st_out[i], 16 * GH * NB // 4)
            product_to_y(G_GLA_O)
            boundary(N_POST_MIX1, R_POST_MIX + 8, 2, N_PRE_MLP1, 4, R_PRE_MLP + 8)
            dve.wait_ge(y_zeroed, 2)
            with dve.Fori(0, 3) as q:
                mlp_up(1, q)
                mlp_down(1, q)
            mlp_up(1, 3)
            for j in range(8):
                add_down(G_MLP[1] + 3 * 16 + 8 + j, 0, j, ahead=j < 6)
            boundary(N_POST_MLP1, R_POST_MLP + 8, 3, None, None, None)
            for i, (t0, n) in enumerate(TILES[1:]):
                dve.wait_ge(y_turned, i + 1)
                if i >= 2:
                    dve.wait_ge(y_out[i % 2], 16 * (i // 2))
                nc.vector.tensor_copy(out_tok[i % 2][0:n, :], psf[0:n, 1024 * (i % 2):1024 * (i % 2) + D]).then_inc(y_placed, 1)

        @block.tensor
        def _(pe):
            def block_product(g, it, ins_hi, ins_lo, ready=None):
                pe.wait_ge(w_split, it * 4 + g + 1)
                if g >= 2:
                    pe.wait_ge(blk_read, it * 4 + g - 1)
                out = ps[:, 2 * (g % 2):2 * (g % 2) + 2, :]
                for c in range(DC):
                    if ready is not None:
                        ready(c)
                    for k, (w, a) in enumerate(((w_hi, ins_hi), (w_hi, ins_lo), (w_lo, ins_hi))):
                        for h in range(2):
                            last = nc.tensor.matmul(out[:, h, 0:HALF], w[g % SPLIT][:, c, :], a[:, c, HALF * h:HALF * h + HALF],
                                                    start=(c == 0 and k == 0), stop=(c == DC - 1 and k == 2))
                last.then_inc(blk_mm, 1)

            def first_blocks(g, fill):
                for b in range(2):
                    pe.wait_ge(w_split, g + b + 1)
                    pe.wait_ge(blk_read, g + b - 1)
                for c in range(DC):
                    pe.wait_ge(act_ready, 8 * fill + c + 1)
                    for b in range(2):
                        for k, (w, a) in enumerate(((w_hi, act_hi), (w_hi, act_lo), (w_lo, act_hi))):
                            for h in range(2):
                                last = nc.tensor.matmul(ps[:, 2 * ((g + b) % 2) + h, 0:HALF], w[(g + b) % SPLIT][:, c, :],
                                                        a[:, c, HALF * h:HALF * h + HALF],
                                                        start=(c == 0 and k == 0), stop=(c == DC - 1 and k == 2))
                        if c == DC - 1:
                            last.then_inc(blk_mm, 1)

            def total(n):
                pe.wait_ge(sq_added, SQ0[n + 1])
                if n:
                    pe.wait_ge(rooted, n)
                for h in range(2):
                    last = nc.tensor.matmul(ps[:, 6 + h, 0:HALF], ones[:], ssum[:, HALF * h:HALF * h + HALF], start=True, stop=True)
                last.then_inc(summed, 1)

            def tail_product(w_a, w_b, m, n):
                pe.wait_ge(tail_split, n)
                for c in range(DC):
                    for k, (w, a) in enumerate(((w_a, act_hi), (w_a, act_lo), (w_b, act_hi))):
                        for h in range(2):
                            last = nc.tensor.matmul(ps[0:m, 4 + h, 0:HALF], w[:, c, :], a[:, c, HALF * h:HALF * h + HALF],
                                                    start=(c == 0 and k == 0), stop=(c == DC - 1 and k == 2))
                last.then_inc(tail_mm, 1)

            pe.sem_inc(p_turned, 2)
            pe.sem_inc(o_mm, 2)
            pe.sem_inc(proj_mm, 1)
            pe.sem_inc(ss_mm, 1)
            pe.sem_inc(sp_turned, 1)
            pe.sem_inc(so_mm, 2)
            pe.wait_ge(const_in, 16)
            pe.wait_ge(gain_in, 16 * 8)
            nc.tensor.transpose(ps[:, 4, 0:N_GAIN], gain_rows[:], ident[0:N_GAIN, 0:N_GAIN]).then_inc(gain_turned, 1)
            for i, (t0, n) in enumerate(TILES):
                if i in (0, 1, NT):
                    pe.wait_ge(x_in[(0, 1, NT).index(i)], 16)
                if i >= 2:
                    pe.wait_ge(x_placed, i - 1)
                for c in range(DC):
                    at = 1024 * (i % 2) + n * c
                    last = nc.tensor.transpose(psf[:, at:at + n], x_tok[0:n, i, P * c:P * c + P], ident[0:n, 0:n])
                last.then_inc(x_turned, 1)
            pe.wait_ge(ones_set, 1)
            pe.wait_ge(x_placed, NT + 1)
            total(N_PRE_MIX0)
            for g in range(4):
                block_product(g, 0, act_hi, act_lo, ready=(lambda c: pe.wait_ge(act_ready, c + 1)) if g == 0 else None)
            tail_product(tail_hi, tail_lo, ROPE, 1)
            rot = cst[0:QH, C_ROT:C_ROT + QH]
            pe.wait_ge(tail_read, 1)
            pe.wait_ge(k_zeroed, 1)
            for h in range(2):
                last = nc.tensor.matmul(ps[0:QH, 4 + h, 0:HALF], rot, kT[:, 0, HALF * h:HALF * h + HALF], start=True, stop=True)
            last.then_inc(krot_mm, 1)
            total(N_CQ)
            total(N_CKV)
            pe.wait_ge(lat_ready, 2 * LC)
            pe.wait_ge(kpe_ready, 1)
            for i, (t0, n) in enumerate(TILES):
                if i >= 2:
                    pe.wait_ge(c_placed, i - 1)
                for c in range(LC):
                    nc.tensor.transpose(ps[0:n, 4 + i % 2, P * c:P * c + P], lat[:, LC + c, t0:t0 + n], ident)
                nc.tensor.transpose(ps[0:n, 4 + i % 2, LORA:LORA + ROPE], kT[NOPE:QH, 0, t0:t0 + n],
                                    ident[NOPE:QH, NOPE:QH]).then_inc(c_turned, 1)
            pe.wait_ge(uv_in, 16)
            pe.wait_ge(blk_read, 4)
            for i, (t0, n) in enumerate(TILES[:NT]):
                if i >= 2:
                    pe.wait_ge(v_placed, i - 1)
                for a in range(2):
                    for c in range(LC):
                        last = nc.tensor.matmul(ps[0:n, 2 * (i % 2) + a, :], lat[:, LC + c, t0:t0 + n], uv[:, c, 512 * a:512 * a + 512],
                                                start=(c == 0), stop=(c == LC - 1))
                last.then_inc(v_mm, 1)
            pe.wait_ge(v_placed, NT)
            pe.wait_ge(c_placed, NT + 1)
            NST = 2 * NT

            def head_scores(p, n):
                hh, i = n // NT, n % NT
                t0, rows = TILES[i]
                pe.wait_ge(exp_done, p * NST + n - 2 + 1 + 2)
                rows = P
                q = qT[hh][:, t0:t0 + rows]
                at = 1024 * (n % 2) + 512
                nc.tensor.matmul(psf[0:rows, at - META:at], q, kT[:, hh, 0:META], start=True, stop=(i > 0))
                if i:
                    nc.tensor.matmul(psf[0:rows, at:at + P * i], q, kT[:, hh, META:META + P * i], start=True, stop=False)
                w = TILES[i][1]
                d = at + P * (i - 1) if i else at - META
                last = nc.tensor.matmul(psf[0:rows, d:d + w], ident, cst[:, C_TRI:C_TRI + w], start=False, stop=True)
                last.then_inc(s_mm, 1)

            def turn_probs(p, n):
                i = n % NT
                pe.wait_ge(exp_done, p * NST + n + 1 + 2)
                pe.wait_ge(p_placed, p * NST + n + 1)
                for k in range(i, -1, -1):
                    t0, nk = TILES[k] if i else (0, P)
                    last = nc.tensor.transpose(psf[0:nk, 2048 + P * k:2048 + P * k + P], prob[n % 3][:, t0:t0 + nk], ident)
                last.then_inc(p_turned, 1)

            def head_out(p, n):
                hh, i = n // NT, n % NT
                pe.wait_ge(p_placed, p * NST + n + 1 + 1)
                pe.wait_ge(o_placed, p * NST + n - 2 + 1 + 2)
                for k in range(i + 1):
                    last = nc.tensor.matmul(ps[:, 6 + n % 2, 0:VH], probT[n % 2][:, k, :],
                                            v[:, k, bass.ds(p * (2 * VH) + hh * VH, VH)], start=(k == 0), stop=(k == i))
                last.then_inc(o_mm, 1)

            with pe.Fori(0, HEADS // 2) as p:
                pe.wait_ge(wk_in, p * 16 + 16)
                for h in range(2):
                    for c in range(LC):
                        last = nc.tensor.matmul(ps[:, h, 0:NP // 2], wk_pair[:, c, :], lat[:, LC + c, NP // 2 * h:NP // 2 * (h + 1)],
                                                start=(c == 0), stop=(c == LC - 1))
                last.then_inc(proj_mm, 1)
                pe.wait_ge(wq_in, p * 16 + 16)
                for hh in range(2):
                    for h in range(2):
                        for c in range(LC):
                            last = nc.tensor.matmul(ps[0:QH, 2 + 2 * hh + h, 0:HALF], wq_pair[:, c, QH * hh:QH * hh + QH],
                                                    lat[:, c, HALF * h:HALF * h + HALF], start=(c == 0), stop=(c == LC - 1))
                    last.then_inc(proj_mm, 1)
                for hh in range(2):
                    pe.wait_ge(q_placed, p * 2 + hh + 1)
                    if hh == 0:
                        pe.wait_ge(o_placed, p * NST + 2)
                    else:
                        pe.wait_ge(k_placed, p * 2 + 2)
                    at = 6 if hh == 0 else 0
                    for h in range(2):
                        last = nc.tensor.matmul(ps[0:QH, at + h, 0:HALF], rot, qT[hh][:, HALF * h:HALF * h + HALF],
                                                start=True, stop=True)
                    last.then_inc(rot_mm, 1)
                pe.wait_ge(q_roped, p * 2 + 2)
                for n in range(NST + 3):
                    if n < NST:
                        head_scores(p, n)
                    if 2 <= n < NST + 2:
                        turn_probs(p, n - 2)
                    if n >= 3:
                        head_out(p, n - 3)
            pe.wait_ge(o_placed, HEADS * NT + 2)
            for i, (t0, n) in enumerate(TILES[:NT]):
                if i >= 2:
                    pe.wait_ge(o_split, i - 1)
                for c in range(DC):
                    at = 1024 * (i % 2) + n * c
                    last = nc.tensor.transpose(psf[:, at:at + n], otok[0:n, i, P * c:P * c + P], ident[0:n, 0:n])
                last.then_inc(o_turned, 1)
            pe.wait_ge(uk_in, 16)
            pe.wait_ge(o_split, NT)
            for k in range(4):
                if k >= 2:
                    pe.wait_ge(uk_placed, k - 1)
                for hh in range(4):
                    for c in range(LC):
                        at = 1024 * (k % 2) + LORA * hh + P * c
                        last = nc.tensor.transpose(psf[0:NOPE, at:at + P], uk[:, c, NOPE * (4 * k + hh):NOPE * (4 * k + hh + 1)], ident)
                last.then_inc(uk_turned, 1)
            pe.wait_ge(uk_placed, 4)
            pe.wait_ge(qs_saved, HEADS + 2)
            for h in range(HEADS):
                for c in range(LC):
                    last = nc.tensor.matmul(ps[:, 4 + c, NSAM * h:NSAM * h + NSAM], ukT[:, h, P * c:P * c + P], qs[0:NOPE, h, :],
                                            start=True, stop=True)
            last.then_inc(qlat_mm, 1)

            def turn_pages(b, s, turn):
                pe.wait_ge(page_in[s], turn * (2 * PAGES * 16) + 2 * PAGES * 16)
                for k in range(3):
                    if not (isinstance(b, int) and b * 3 + k < 2):
                        pe.wait_ge(pg_placed, b * 3 + k - 1)
                    for g in range(PAGES):
                        at = 1024 * ((s + k) % 2) + P * g
                        if k < LC:
                            last = nc.tensor.transpose(psf[:, at:at + P], pg_ckv[s][:, g, P * k:P * k + P], ident)
                        else:
                            last = nc.tensor.transpose(psf[0:ROPE, at:at + P], pg_kpe[s][:, g, :], ident)
                    last.then_inc(pg_turned, 1)

            def sample_attention(b, s, turn, last_one=False):
                rows = HEADS * NS
                pe.wait_ge(qcur_ready, b + 2)
                pe.wait_ge(pg_placed, b * 3 + 3)
                pe.wait_ge(ss_exp, b + 1)
                for a in range(2):
                    for c in range(LC):
                        nc.tensor.matmul(ps[0:rows, 4 + a, :], qcur[s][:, c, :], ckT[:, c, 512 * a:512 * a + 512],
                                         start=(c == 0), stop=False)
                    nc.tensor.matmul(ps[0:rows, 4 + a, :], qpcur[s][:], kpT[:, 512 * a:512 * a + 512], start=False, stop=True)
                pe.wait_ge(so_placed, b + 1)
                for c in range(LC):
                    nc.tensor.matmul(ps[0:rows, 6, 0:NSAM], qcur[s][:, c, :], lat[:, LC + c, NP:T], start=(c == 0), stop=False)
                nc.tensor.matmul(ps[0:rows, 6, 0:NSAM], qpcur[s][:], kpe_new[:], start=False, stop=True).then_inc(ss_mm, 1)
                if not last_one:
                    turn_pages(b + 1, 1 - s, turn + s)
                pe.wait_ge(ss_norm, b + 1)
                pe.wait_ge(sp_placed, b + 1)
                nc.tensor.transpose(ps[:, 7, 0:P], sprob[:, 0:P], ident)
                for g in range(1, PAGES):
                    nc.tensor.transpose(ps[:, 7, rows * g:rows * g + rows], sprob[0:rows, P * g:P * g + P], ident[0:rows, 0:rows])
                last = nc.tensor.transpose(ps[0:NSAM, 6, P:P + rows], sprob[0:rows, PAST:PAST + NSAM], ident[0:rows, 0:rows])
                last.then_inc(sp_turned, 1)
                pe.wait_ge(sp_placed, b + 1 + 1)
                for c in range(LC):
                    out = ps[:, 6, 256 + rows * c:256 + rows * (c + 1)]
                    for g in range(PAGES):
                        nc.tensor.matmul(out, pg_ckv[s][:, g, P * c:P * c + P], sprobT[:, g, :], start=(g == 0), stop=False)
                    last = nc.tensor.matmul(out, ctok[0:NSAM, NT, P * c:P * c + P], sprobN[:], start=False, stop=True)
                last.then_inc(so_mm, 1)

            pe.wait_ge(qlat_ready, 4)
            turn_pages(0, 0, 0)
            with pe.Fori(0, NB // 2 - 1) as i:
                for s in range(2):
                    sample_attention(i * 2 + s, s, i)
            for s in range(2):
                sample_attention(NB - 2 + s, s, NB // 2 - 1, last_one=(s == 1))
            pe.wait_ge(so_placed, NB + 1)
            for h in range(HEADS):
                for c in range(LC):
                    last = nc.tensor.matmul(ps[VH * (h % 2):VH * (h % 2) + VH, 0, NSAM * (h // 2):NSAM * (h // 2) + NSAM],
                                            uv[:, c, VH * h:VH * h + VH], olat[:, c, h, :], start=(c == 0), stop=(c == LC - 1))
            last.then_inc(o_turned, 1)
            pe.wait_ge(o_split, NT + 1)
            with pe.Fori(0, 2) as it:
                for j in range(4):
                    block_product(G_MLA_O + j, it, act_hi, act_lo)

            def mlp_up(layer, q):
                with pe.Fori(0, 2) as it:
                    for j in range(4):
                        block_product(G_MLP[layer] + j, q * 4 + it, act_hi, act_lo)

            def mlp_down(layer, q):
                with pe.Fori(0, 2) as it:
                    for j in range(4):
                        block_product(G_MLP[layer] + 8 + j, q * 4 + it, h_hi, h_lo,
                                      ready=(lambda c: pe.wait_ge(h_ready, q * 8 + layer * 32 + c + 1 + 2)) if j == 0 else None)

            def boundary(n_out, n_in, fill, g):
                total(n_out)
                first_blocks(g, fill)
                total(n_in)
                for j in range(2, 4):
                    block_product(g + j, 0, act_hi, act_lo)

            def mlp(layer):
                for j in range(4):
                    block_product(G_MLP[layer] + j, 1, act_hi, act_lo)
                mlp_down(layer, 0)
                with pe.Fori(1, 4) as q:
                    mlp_up(layer, q)
                    mlp_down(layer, q)

            boundary(N_POST_MIX0, N_PRE_MLP0, 1, G_MLP[0])
            mlp(0)
            boundary(N_POST_MLP0, N_PRE_MIX1, 2, G_GLA_IN)
            for j in range(4):
                block_product(G_GLA_IN + j, 1, act_hi, act_lo)
            with pe.Fori(0, 2) as it:
                for j in range(4):
                    block_product(G_GLA_IN + 8 + j, it, act_hi, act_lo)
                pe.wait_ge(blk_read, it * 4 + G_GLA_IN + 8 + 4)
                for i, (t0, n) in enumerate(TILES):
                    if i >= 2:
                        pe.wait_ge(gv_placed, it * (NT + 1) + i - 1)
                    for j in range(4):
                        last = nc.tensor.transpose(ps[0:n, 4 + i % 2, P * j:P * j + P], vT[j][:, t0:t0 + n], ident)
                    last.then_inc(v_turned, 1)
            with pe.Fori(0, 2) as it:
                for j in range(4):
                    block_product(G_GLA_IN + 16 + j, it, act_hi, act_lo)
            tail_product(gd_hi, gd_lo, RANK, 2)
            pe.wait_ge(gdT_ready, 1)
            pe.wait_ge(wg_in, 16)
            pe.wait_ge(blk_read, G_GLA_IN + 24)
            for h in range(GH):
                gq, gk = gqk[:, h, :], gqk[:, GH + h, :]
                if h:
                    pe.wait_ge(st_ready, NB * h)
                for a in range(2):
                    last = nc.tensor.matmul(ps[:, 4 + a, 0:HALF], wg[:, GK * h:GK * h + GK], gdT[:, HALF * a:HALF * a + HALF],
                                            start=True, stop=True)
                last.then_inc(gate_mm, 1)
                pe.wait_ge(gla_step, GLA_STEPS * h + 9)
                for i, (t0, n) in enumerate(TILES):
                    last = nc.tensor.transpose(psf[0:n, 2048 + GK * i:2048 + GK * i + GK], tA[:, t0:t0 + n], ident)
                last.then_inc(kd_turned, 1)
                pe.wait_ge(kd_placed, h + 1)
                pe.wait_ge(rooted, N_GLA + h)
                if h:
                    pe.wait_ge(og_placed, 2 * h)

                def chunk_out(c):
                    base, n, t0, tile = chunk_at(c)
                    k = h * NCH + c
                    pe.wait_ge(att_ready, k + 1)
                    if c:
                        pe.wait_ge(state_ready, k)
                    for a in range(2):
                        at = 1024 * a + OG0 + t0
                        last = nc.tensor.matmul(psf[:, at:at + n], gv[:, tile, GV * h + P * a:GV * h + P * a + P],
                                                attT[:, att_slot(c), 0:n], start=True, stop=(c == 0))
                        if c:
                            last = nc.tensor.matmul(psf[:, at:at + n], stp[(c - 1) % 2][:, P * a:P * a + P], gq[:, t0:t0 + n],
                                                    start=False, stop=True)
                    last.then_inc(og_mm, 1)

                for c in range(NCH):
                    base, n, t0, tile = chunk_at(c)
                    k = h * NCH + c
                    if c >= 2:
                        pe.wait_ge(att_ready, k - 1)
                    nc.tensor.matmul(ps[base:base + n, ATT_BANK[c % 2], 0:n], gk[:, t0:t0 + n], gq[:, t0:t0 + n], start=True, stop=True)\
                        .then_inc(att_mm, 1)
                    if c >= 2:
                        pe.wait_ge(state_ready, k - 1)
                    nc.tensor.matmul(ps[:, 5 + c % 2, 0:GV], kd_tok[base:base + n, tile, :],
                                     gv[base:base + n, tile, GV * h:GV * h + GV], start=True, stop=True).then_inc(up_mm, 1)
                    if c >= 1:
                        chunk_out(c - 1)
                chunk_out(NCH - 1)
                nc.tensor.matmul(ps[0:NSAM, 4, P:P + NSAM], gk[:, NP:T], gq[:, NP:T], start=True, stop=True).then_inc(satt_mm, 1)
                pe.wait_ge(satt_ready, h + 1)
                pe.wait_ge(kdb_ready, h + 1)
                pe.wait_ge(state_ready, NCH * (h + 1))
                for a in range(2):
                    at = 1024 * a + OG0 + NP
                    nc.tensor.matmul(psf[:, at:at + NSAM], gv[0:NSAM, NT, GV * h + P * a:GV * h + P * a + P], attS[:],
                                     start=True, stop=False)
                for b in range(NB):
                    k = h * NB + b
                    pe.wait_ge(st_in[k % 4], 16 * (k // 4 + 1))
                    for a in range(2):
                        at = 1024 * a + OG0 + NP + NS * b
                        nc.tensor.matmul(psf[:, at:at + NS], sts[k % 4][:, P * a:P * a + P], gq[:, NP + NS * b:NP + NS * b + NS],
                                         start=False, stop=(b == NB - 1))
                    if b >= 2:
                        pe.wait_ge(st_ready, k - 1)
                    nc.tensor.matmul(ps[:, 5 + b % 2, 0:GV], kd_b[:, b, :], gv[0:NSAM, NT, GV * h:GV * h + GV],
                                     start=True, stop=True).then_inc(sup_mm, 1)
                total(N_GLA + h)
            pe.wait_ge(act_ready, 8 * 4)
            pe.wait_ge(og_placed, 2 * GH)
            with pe.Fori(0, 2) as it:
                for j in range(4):
                    block_product(G_GLA_O + j, it, act_hi, act_lo)
            boundary(N_POST_MIX1, N_PRE_MLP1, 4, G_MLP[1])
            mlp(1)
            total(N_POST_MLP1)
            pe.wait_ge(x_updated, 8 * 4)
            pe.wait_ge(blk_read, G_END)
            for i, (t0, n) in enumerate(TILES[1:]):
                if i >= 2:
                    pe.wait_ge(y_placed, i - 1)
                for c in range(DC):
                    at = 1024 * (i % 2) + P * c
                    last = nc.tensor.transpose(psf[0:n, at:at + P], x[:, c, t0:t0 + n], ident)
                last.then_inc(y_turned, 1)


_INS = ['x_prompt', 'x_sample', 'cache_ckv', 'cache_kpe', 'state_gla', 'page_table', 'meta_tokens', 'norm_pre_mix',
        'norm_post_mix', 'norm_pre_mlp', 'norm_post_mlp', 'mla_w_in', 'mla_q_norm', 'mla_w_uq', 'mla_kv_norm',
        'mla_w_uk', 'mla_w_uv', 'mla_w_o', 'gla_w_in', 'gla_w_gate', 'gla_b_gate', 'gla_norm', 'gla_w_o',
        'mlp_w_up', 'mlp_w_down']
_OUTS = [(1, SEQ, D), (NB, NS, D), (1, 1, NP, LORA), (1, 1, NP, ROPE), (1, NB, NS, LORA), (1, NB, NS, ROPE),
         (1, 1, GH, GK, GV), (1, NB, GH, GK, GV)]


def kernel(**inputs):
    import numpy as _np
    import concourse.bacc as _bacc
    from concourse import mybir as _mybir
    from concourse.bass_utils import run_bass_kernel_spmd as _run

    nc = _bacc.Bacc("TRN2", target_bir_lowering=False, num_devices=1)
    arrays, args = {}, []
    for name in _INS:
        a = _np.ascontiguousarray(inputs[name])
        arrays[f"in_{name}_dram"] = a
        args.append(nc.dram_tensor(f"in_{name}_dram", a.shape, _mybir.dt.from_np(a.dtype), kind="ExternalInput").ap())
    arrays["const_dram"] = constants()
    args.append(nc.dram_tensor("const_dram", (P, N_CONST), _mybir.dt.float32, kind="ExternalInput").ap())
    for i, shape in enumerate(_OUTS):
        args.append(nc.dram_tensor(f"out_{i}_dram", shape, _mybir.dt.float32, kind="ExternalOutput").ap())
    trunk(nc, *args)
    r = _run(nc, [arrays], core_ids=[0])
    return tuple(r.results[0][f"out_{i}_dram"] for i in range(len(_OUTS)))
```

```python
from contextlib import ExitStack

import numpy as np
import concourse.bass as bass
from concourse import mybir

F32 = mybir.dt.float32
F32R = mybir.dt.float32r
I32 = mybir.dt.int32
ALU = mybir.AluOpType
ACT = mybir.ActivationFunctionType
AX_X = mybir.AxisListType.X

P = 128
D = 1024
DC = D // P
META, SEQ, NB, NS = 16, 512, 8, 4
NP = META + SEQ
NSAM = NB * NS
T = NP + NSAM
HALF = T // 2
FF = 4 * D
HEADS, NOPE, ROPE, VH = 16, 64, 32, 64
QH = NOPE + ROPE
LORA = 256
LC = LORA // P
PAGE = 128
PAGES = 8
PAST = PAGE * PAGES
SCALE = QH ** -0.5
GH, GK, GV = 4, 128, 256
GSCALE = GK ** -0.5
TAU = 16.0
RANK = 16
CH = 64
EPS = 1e-6
PIECES = 6
GLA_STEPS = 12
NST_S = 2

TILES = [(0, META)] + [(META + P * i, P) for i in range(SEQ // P)] + [(NP, NSAM)]
NT = len(TILES) - 1

NCH = 1 + SEQ // CH
ATT_BANK = (4, 7)


def chunk_at(c):
    if c == 0:
        return 0, META, 0, 0
    return CH * ((c - 1) % 2), CH, META + CH * (c - 1), 1 + (c - 1) // 2


G_MLA_IN = 0
G_MLA_O = G_MLA_IN + 4
G_MLP = [G_MLA_O + 8, 0]
G_GLA_IN = G_MLP[0] + 64
G_GLA_O = G_GLA_IN + 24
G_MLP[1] = G_GLA_O + 8
G_END = G_MLP[1] + 64
RAW, SPLIT = 4, 2
PG_S = 3

R_PRE_MIX, R_POST_MIX, R_PRE_MLP, R_POST_MLP = 0, 16, 32, 48
R_Q, R_KV, R_GLA, R_BG = 64, 66, 68, 70
N_GAIN = 74

NORMS = [(8, D), (2, LORA), (2, LORA), (8, D), (8, D), (8, D), (8, D)] + [(2, GV)] * GH + [(8, D)] * 3
(N_PRE_MIX0, N_CQ, N_CKV, N_POST_MIX0, N_PRE_MLP0, N_POST_MLP0, N_PRE_MIX1, N_GLA, _, _, _,
 N_POST_MIX1, N_PRE_MLP1, N_POST_MLP1) = range(14)
SQ0 = [sum(c for c, _ in NORMS[:n]) for n in range(len(NORMS) + 1)]

C_ID = 0
C_ROT = C_ID + P
C_COS = C_ROT + QH
C_SIN = C_COS + T
C_TRI = C_SIN + T
C_SMASK = C_TRI + P
C_GTRI = C_SMASK + NB * NSAM
C_GSAM = C_GTRI + CH
C_GBM = C_GSAM + NSAM
C_SCAN = C_GBM + NB
N_CONST = C_SCAN + T


def att_slot(c):
    return 0 if c == 0 else 2 - c % 2


def constants():
    c = np.zeros((P, N_CONST), np.float32)
    c[:, C_ID:C_ID + P] = np.eye(P)
    h = ROPE // 2
    rot = np.zeros((ROPE, ROPE), np.float32)
    rot[h + np.arange(h), np.arange(h)] = -1.0
    rot[np.arange(h), h + np.arange(h)] = 1.0
    pos = np.concatenate([np.arange(NP), np.tile(PAST + np.arange(NS), NB)]).astype(np.float32)
    inv = (np.float32(10000.0) ** (-np.arange(h, dtype=np.float32) / np.float32(h))).astype(np.float32)
    ang = (pos[None, :] * inv[:, None]).astype(np.float32)
    c[NOPE:QH, C_ROT + NOPE:C_ROT + QH] = rot
    c[NOPE:QH, C_COS:C_COS + T] = np.tile(np.cos(ang), (2, 1))
    c[NOPE:QH, C_SIN:C_SIN + T] = np.tile(np.sin(ang), (2, 1))
    i = np.arange(P)
    c[:, C_TRI:C_TRI + P] = np.where(i[None, :] <= i[:, None], 0.0, -1e30)
    s = np.arange(NSAM)
    for b in range(NB):
        ok = (s[None, :] // NS == b) & (s[None, :] % NS <= np.arange(HEADS * NS)[:, None] % NS)
        c[0:HEADS * NS, C_SMASK + b * NSAM:C_SMASK + (b + 1) * NSAM] = np.where(ok, 0.0, -1e30)
    j = np.arange(P) % CH
    c[:, C_GTRI:C_GTRI + CH] = np.where(j[:, None] <= np.arange(CH)[None, :], 1.0, 0.0)
    c[0:NSAM, C_GSAM:C_GSAM + NSAM] = np.where((s[:, None] // NS == s[None, :] // NS) & (s[:, None] <= s[None, :]), 1.0, 0.0)
    c[0:NSAM, C_GBM:C_GBM + NB] = np.where(s[:, None] // NS == np.arange(NB)[None, :], 1.0, 0.0)
    scan = np.ones(T, np.float32)
    scan[[0] + [META + CH * k for k in range(SEQ // CH)] + [NP + NS * b for b in range(NB)]] = 0.0
    c[:, C_SCAN:] = scan[None, :]
    return c


def trunk(nc, x_prompt, x_sample, cache_ckv, cache_kpe, state_gla, page_table, meta_tokens, norm_pre_mix,
          norm_post_mix, norm_pre_mlp, norm_post_mlp, mla_w_in, mla_q_norm, mla_w_uq, mla_kv_norm, mla_w_uk,
          mla_w_uv, mla_w_o, gla_w_in, gla_w_gate, gla_b_gate, gla_norm, gla_w_o, mlp_w_up, mlp_w_down, const,
          y_prompt, y_sample, new_ckv_prompt, new_kpe_prompt, new_ckv_sample, new_kpe_sample, new_gla_prompt,
          new_gla_sample):
    ctx = ExitStack()
    with ctx:
        def sb_in(scope, name, shape, dt=F32):
            return scope.enter_context(nc.sbuf_tensor(name, shape, dt))

        def sb(name, shape, dt=F32):
            return sb_in(ctx, name, shape, dt)

        def sem(name):
            return ctx.enter_context(nc.semaphore(name))

        cst = sb("cst", [P, N_CONST])
        gain = sb("gain", [P, N_GAIN])
        ones = sb("ones", [P, P])
        eps = sb("eps", [P, 1])
        x = sb("x", [P, DC, T])
        with ExitStack() as s:
            act_hi = sb_in(s, "act_hi", [P, DC, T], F32R)
            act_lo = sb_in(s, "act_lo", [P, DC, T], F32R)
        with ExitStack() as s:
            kd_tok = sb_in(s, "kd_tok", [P, NT + 1, GH * GK])
            attT = sb_in(s, "attT", [P, 3, GH, CH])
            sb_in(s, "act_gap", [P, DC * T - (NT + 1) * GH * GK - 3 * GH * CH])
            og = sb_in(s, "og", [P, DC, T])
        with ExitStack() as s:
            uk = sb_in(s, "uk", [P, LC, HEADS * NOPE])
            ukT = sb_in(s, "ukT", [NOPE, HEADS, LORA])
        sb("act_region", [P, 2 * DC * T])
        w_raw = [sb(f"w_raw{i}", [P, DC, P]) for i in range(RAW)]
        w_hi = [sb(f"w_hi{i}", [P, DC, P], F32R) for i in range(SPLIT)]
        w_lo = [sb(f"w_lo{i}", [P, DC, P], F32R) for i in range(SPLIT)]
        rstd_pre = sb("rstd_pre", [P, T])
        rstd_post = sb("rstd_post", [P, T])
        ssum = sb("ssum", [P, T])
        std = sb("std", [P, T])
        sq = [sb(f"sq{i}", [P, T]) for i in range(2)]

        with ExitStack() as s:
            x_tok = sb_in(s, "x_tok", [P, NT + 1, D])
            gain_rows = sb_in(s, "gain_rows", [N_GAIN, P])

        with ExitStack() as s:
            tail_raw = sb_in(s, "kpe_w_raw", [P, DC, ROPE])
            tail_hi = sb_in(s, "kpe_w_hi", [P, DC, ROPE], F32R)
            tail_lo = sb_in(s, "kpe_w_lo", [P, DC, ROPE], F32R)
            lat = sb_in(s, "lat", [P, 2 * LC, T])
            kT = sb_in(s, "kT", [QH, 2, T])
            uv = sb_in(s, "uv", [P, LC, HEADS * VH])
            qs = sb_in(s, "qs", [QH, HEADS, NSAM])
            ctok = sb_in(s, "ctok", [P, NT + 1, LORA + ROPE])
            pages = sb_in(s, "pages", [1, NB * PAGES], I32)
            with ExitStack() as s2:
                rope_tmp = sb_in(s2, "rope_tmp", [QH, T])
                v = sb_in(s2, "v", [P, NT, HEADS * VH])
                otok = sb_in(s2, "otok", [P, NT, HEADS * VH])
                qT = [sb_in(s2, f"qT{i}", [QH, T]) for i in range(2)]
                wq_head = [sb_in(s2, f"wq_head{i}", [P, LC, QH]) for i in range(2)]
                wk_head = [sb_in(s2, f"wk_head{i}", [P, LC, NOPE]) for i in range(2)]
                prob = [sb_in(s2, f"prob{i}", [P, NP]) for i in range(3)]
                probT = [sb_in(s2, f"probT{i}", [P, NT, P]) for i in range(2)]
                stat = sb_in(s2, "stat", [P, 3, 2 * NT])
            with ExitStack() as s2:
                qlat = sb_in(s2, "qlat", [P, LC, NB, HEADS * NS])
                qpe = sb_in(s2, "qpe", [ROPE, NB, HEADS * NS])
                kpe_new = sb_in(s2, "kpe_new", [ROPE, NSAM])
                olat = sb_in(s2, "olat", [P, LC, HEADS, NSAM])
                with ExitStack() as s3:
                    pg_ckv, pg_kpe = zip(*[(sb_in(s3, f"pg_ckv{i}", [P, PAGES, LORA]),
                                            sb_in(s3, f"pg_kpe{i}", [P, PAGES, ROPE])) for i in range(PG_S)])
                    ckT = sb_in(s3, "ckT", [P, LC, PAST])
                    kpT = sb_in(s3, "kpT", [ROPE, PAST])
                    qcur = sb_in(s3, "qcur", [P, LC, HEADS * NS])
                    qpcur = sb_in(s3, "qpcur", [ROPE, HEADS * NS])
                    sprob = sb_in(s3, "sprob", [P, PAST + NSAM])
                    sprobT = sb_in(s3, "sprobT", [P, PAGES, HEADS * NS])
                    sprobN = sb_in(s3, "sprobN", [NSAM, HEADS * NS])
                    sstat = sb_in(s3, "sstat", [HEADS * NS, 3])

        with ExitStack() as s:
            y = sb_in(s, "y", [P, DC, T])
            h_hi = sb_in(s, "h_hi", [P, DC, T], F32R)
            h_lo = sb_in(s, "h_lo", [P, DC, T], F32R)
            relu = [sb_in(s, f"relu{i}", [P, T]) for i in range(2)]
            relu2 = sb_in(s, "relu2", [P, T])
            out_tok = [sb_in(s, f"out_tok{i}", [P, D]) for i in range(NT)]

        with ExitStack() as s:
            gqk = sb_in(s, "gqk", [P, 2 * GH, T])
            gr = sb_in(s, "gr", [P, DC, T])
            gv = sb_in(s, "gv", [P, NT + 1, GH * GV])
            vT = [sb_in(s, f"vT{i}", [P, T]) for i in range(4)]
            tmp = [sb_in(s, f"gla_tmp{i}", [P, T]) for i in range(4)]
            tA, tB, tC, bcum = tmp
            decay = sb_in(s, "decay", [P, GH, NCH + NB])
            kd_b = [sb_in(s, f"kd_b{i}", [NSAM, GH * GK]) for i in range(2)]
            attS = sb_in(s, "attS", [NSAM, GH, NSAM])
            with ExitStack() as s2:
                gd_raw = sb_in(s2, "gd_raw", [P, DC, RANK])
                gd_hi = sb_in(s2, "gd_hi", [P, DC, RANK], F32R)
                gd_lo = sb_in(s2, "gd_lo", [P, DC, RANK], F32R)
                gdT = sb_in(s2, "gdT", [RANK, T])
                wg = sb_in(s2, "wg", [RANK, GH * GK])
            with ExitStack() as s2:
                stp = [sb_in(s2, f"stp{i}", [P, GH, GV]) for i in range(2)]
                sts = [sb_in(s2, f"sts{i}", [P, GH, GV]) for i in range(NST_S)]

        ps = ctx.enter_context(nc.psum_tensor("ps", [P, 8, 512], F32))
        psf = ps[:, :, :].rearrange("p b n -> p (b n)")

        def blk_ps(g):
            return ps[:, 2 * (g % 2):2 * (g % 2) + 2, 0:HALF]

        def x_wait(eng, u, c):
            eng.wait_ge(x_updated[c % 2], DC // 2 * u + c // 2 + 1)

        def halves(ap):
            return ap.rearrange("p (h n) -> p h n", h=2)

        def chunk(ap):
            return ap.rearrange("p (o n) -> p o n", o=1)

        NORM_PS = ps[:, 6:8, 0:HALF]
        ident = cst[:, C_ID:C_ID + P]

        const_in = sem("const_in")
        gain_in = sem("gain_in")
        x_in = [sem(f"x_in{i}") for i in range(3)]
        ones_set = sem("ones_set")
        gain_turned = sem("gain_turned")
        gain_placed = sem("gain_placed")
        x_turned = sem("x_turned")
        x_placed = sem("x_placed")
        w_loaded = [sem(f"w_loaded{i}") for i in range(RAW)]
        w_rounded = sem("w_rounded")
        w_split = sem("w_split")
        blk_mm = sem("blk_mm")
        blk_read = sem("blk_read")
        squared = sem("squared")
        sq_added = sem("sq_added")
        summed = sem("summed")
        rooted = sem("rooted")
        inverted = sem("inverted")
        act_rounded = sem("act_rounded")
        act_ready = sem("act_ready")
        y_normed = sem("y_normed")
        x_updated = [sem(f"x_updated{i}") for i in range(2)]
        y_zeroed = sem("y_zeroed")
        h_rounded = sem("h_rounded")
        relu_squared = sem("relu_squared")
        h_ready = sem("h_ready")
        tail_in = sem("tail_in")
        tail_rounded = sem("tail_rounded")
        tail_split = sem("tail_split")
        tail_mm = sem("tail_mm")
        tail_read = sem("tail_read")
        krot_mm = sem("krot_mm")
        kpe_step = sem("kpe_step")
        kpe_ready = sem("kpe_ready")
        k_zeroed = sem("k_zeroed")
        att_zeroed = sem("att_zeroed")
        att_cleared = sem("att_cleared")
        lat_ready = sem("lat_ready")
        uv_in = sem("uv_in")
        pages_in = sem("pages_in")
        c_turned = sem("c_turned")
        c_placed = sem("c_placed")
        v_mm = sem("v_mm")
        v_placed = sem("v_placed")
        wq_in = [sem(f"wq_in{i}") for i in range(2)]
        wk_in = [sem(f"wk_in{i}") for i in range(2)]
        piece_mm = sem("piece_mm")
        k_placed = sem("k_placed")
        q_placed = sem("q_placed")
        rope_step = sem("rope_step")
        q_roped = sem("q_roped")
        qs_saved = sem("qs_saved")
        s_mm = sem("s_mm")
        bias_ready = sem("bias_ready")
        exp_done = sem("exp_done")
        p_turned = sem("p_turned")
        p_placed = sem("p_placed")
        p_first = sem("p_first")
        rsum_inv = sem("rsum_inv")
        o_mm = sem("o_mm")
        o_placed = sem("o_placed")
        o_turned = sem("o_turned")
        o_rounded = sem("o_rounded")
        o_split = sem("o_split")
        uk_in = sem("uk_in")
        uk_turned = sem("uk_turned")
        uk_placed = sem("uk_placed")
        qlat_mm = sem("qlat_mm")
        qlat_ready = sem("qlat_ready")
        page_in = [sem(f"page_in{i}") for i in range(PG_S)]
        pg_turned = sem("pg_turned")
        pg_placed = sem("pg_placed")
        pg1_placed = sem("pg1_placed")
        qcur_ready = sem("qcur_ready")
        ss_mm = sem("ss_mm")
        ss_step = sem("ss_step")
        ss_bias = sem("ss_bias")
        ss_exp = sem("ss_exp")
        ss_norm = sem("ss_norm")
        sp_turned = sem("sp_turned")
        sp_placed = sem("sp_placed")
        so_mm = sem("so_mm")
        so_placed = sem("so_placed")
        gd_in = sem("gd_in")
        v_turned = sem("v_turned")
        gv_placed = sem("gv_placed")
        silu_done = sem("silu_done")
        og_normed = sem("og_normed")
        og_gated = sem("og_gated")
        gate_mm = sem("gate_mm")
        gdT_ready = sem("gdT_ready")
        wg_in = sem("wg_in")
        gla_step = sem("gla_step")
        gla_act = sem("gla_act")
        kd_turned = sem("kd_turned")
        kd_placed = sem("kd_placed")
        kdb_ready = sem("kdb_ready")
        att_mm = sem("att_mm")
        att_ready = sem("att_ready")
        up_mm = sem("up_mm")
        state_ready = sem("state_ready")
        og_mm = sem("og_mm")
        og_placed = sem("og_placed")
        satt_mm = sem("satt_mm")
        satt_ready = sem("satt_ready")
        st_in = [sem(f"st_in{i}") for i in range(NST_S)]
        sup_mm = sem("sup_mm")
        st_ready = sem("st_ready")
        st_out = [sem(f"st_out{i}") for i in range(NST_S)]
        gp_out = sem("gp_out")
        y_turned = sem("y_turned")
        y_placed = [sem(f"y_placed{i}") for i in range(2)]
        y_out = [sem(f"y_out{i}") for i in range(2)]
        c_out = sem("c_out")

        uq_v = mla_w_uq[0].rearrange("(c p) n -> p c n", p=P)
        uk_v = mla_w_uk[0].rearrange("(c p) h n -> p c (h n)", p=P)
        uv_v = mla_w_uv[0].rearrange("(c p) h n -> p c (h n)", p=P)

        def cols(w, at):
            return w.rearrange("(c p) m -> p c m", p=P)[:, :, bass.ds(at, P)]

        def raw_slot(g):
            return g % RAW

        block = ctx.enter_context(nc.Block())

        @block.sync
        def _(sp):
            def load_block(src, g, it=0):
                if g >= RAW:
                    sp.wait_ge(w_split, it * 4 + g - RAW + 1)
                sp.dma_start(w_raw[raw_slot(g)][:], src).then_inc(w_loaded[raw_slot(g)], 16)

            sp.dma_start(x_tok[0:META, 0, :], meta_tokens).then_inc(x_in[0], 16)
            sp.dma_start(x_tok[:, 1:NT, :], x_prompt[0].rearrange("(i p) d -> p i d", p=P)).then_inc(x_in[1], 16)
            sp.dma_start(x_tok[0:NSAM, NT, :], x_sample.rearrange("b s d -> (b s) d")).then_inc(x_in[2], 16)
            for g in range(4):
                load_block(cols(mla_w_in[0], g * P), G_MLA_IN + g)
            for j in range(4):
                load_block(cols(mla_w_o[0], j * P), G_MLA_O + j)
            sp.wait_ge(pages_in, 16)
            sp.wait_ge(o_placed, HEADS * NT + 2)

            def load_pages(b, s):
                at = [sp.value_load(pages[0:1, bass.ds(b * PAGES + g, 1)], min_val=0,
                                    max_val=cache_ckv.shape[1] - 1) for g in range(PAGES)]
                sp.wait_ge(so_mm, b + 1)
                if s:
                    sp.wait_ge(o_turned, NT)
                for g, n in enumerate(at):
                    sp.dma_start(pg_ckv[s][:, g, :], cache_ckv[0][bass.ds(n, 1)].rearrange("a p c -> p (a c)"))\
                        .then_inc(page_in[s], 16)
                    sp.dma_start(pg_kpe[s][:, g, :], cache_kpe[0][bass.ds(n, 1)].rearrange("a p c -> p (a c)"))\
                        .then_inc(page_in[s], 16)

            with sp.Fori(0, NB // PG_S) as i:
                for s in range(PG_S):
                    load_pages(i * PG_S + s, s)
            for b in range(NB // PG_S * PG_S, NB):
                load_pages(b, b % PG_S)
            for j in range(4, 8):
                load_block(cols(mla_w_o[0], j * P), G_MLA_O + j)

            def mlp(layer):
                with sp.Fori(0, 4) as q:
                    with sp.Fori(0, 2) as it:
                        for j in range(4):
                            load_block(cols(mlp_w_up[layer], q * D + it * (4 * P) + j * P),
                                       G_MLP[layer] + j, q * 4 + it)
                    with sp.Fori(0, 2) as it:
                        for j in range(4):
                            load_block(cols(mlp_w_down[layer][bass.ds(q * D, D), :], it * (4 * P) + j * P),
                                       G_MLP[layer] + 8 + j, q * 4 + it)

            mlp(0)
            with sp.Fori(0, 6) as it:
                for j in range(4):
                    load_block(cols(gla_w_in[0], it * (4 * P) + j * P), G_GLA_IN + j, it)
            with sp.Fori(0, 2) as it:
                for j in range(4):
                    load_block(cols(gla_w_o[0], it * (4 * P) + j * P), G_GLA_O + j, it)
            mlp(1)
            for i, (t0, n) in enumerate(TILES[1:]):
                sp.wait_ge(y_placed[i % 2], i // 2 + 1)
                dst = y_prompt[0, t0 - META:t0 - META + n, :] if i < NT - 1 else y_sample.rearrange("b s d -> (b s) d")
                sp.dma_start(dst, out_tok[i][0:n, :]).then_inc(y_out[i % 2], 16)
            sp.wait_ge(y_out[0], 16 * 3)
            sp.wait_ge(y_out[1], 16 * 2)

        @block.gpsimd
        def _(pool):
            pool.dma_start(cst[:], const).then_inc(const_in, 16)
            for r, w in ((R_PRE_MIX, norm_pre_mix), (R_POST_MIX, norm_post_mix), (R_PRE_MLP, norm_pre_mlp),
                         (R_POST_MLP, norm_post_mlp)):
                pool.dma_start(gain_rows[r:r + 16, :], w.rearrange("l (c p) -> (l c) p", p=P)).then_inc(gain_in, 16)
            for r, w in ((R_Q, mla_q_norm), (R_KV, mla_kv_norm), (R_GLA, gla_norm), (R_BG, gla_b_gate)):
                k = w.shape[1] // P
                pool.dma_start(gain_rows[r:r + k, :], w.rearrange("l (c p) -> (l c) p", p=P)).then_inc(gain_in, 16)
            pool.dma_start(pages[:], page_table.rearrange("(o b) n -> o (b n)", o=1)).then_inc(pages_in, 16)
            nc.gpsimd.memset(ones[:], 1.0)
            nc.gpsimd.memset(eps[:], EPS).then_inc(ones_set, 1)
            pool.sem_inc(h_ready, 2)
            pool.sem_inc(qs_saved, 2)

            def add_square(n, c):
                k = SQ0[n] + c
                pool.wait_ge(squared, k + 1)
                if c == 0:
                    if n:
                        pool.wait_ge(summed, n)
                    nc.gpsimd.tensor_copy(ssum[:], sq[k % 2][:]).then_inc(sq_added, 1)
                else:
                    pool.wait_ge(sq_added, k)
                    nc.gpsimd.tensor_tensor(ssum[:], ssum[:], sq[k % 2][:], ALU.add).then_inc(sq_added, 1)

            def add_squares(n):
                for c in range(NORMS[n][0]):
                    add_square(n, c)

            def boundary(n_out, u, n_in=None):
                add_squares(n_out)
                for c in range(0, DC, 2):
                    pool.wait_ge(y_normed, 8 * u + c + 1)
                    nc.gpsimd.tensor_tensor(x[:, c, :], x[:, c, :], y[:, c, :], ALU.add).then_inc(x_updated[0], 1)
                    if c and n_in is not None:
                        add_square(n_in, c - 2)
                        add_square(n_in, c - 1)
                if n_in is not None:
                    add_square(n_in, DC - 2)
                    add_square(n_in, DC - 1)

            def mlp(layer):
                with pool.Fori(0, 4) as q:
                    with pool.Fori(0, 2) as it:
                        for j in range(4):
                            g = G_MLP[layer] + j + q * 16 + it * 4
                            n = layer * 32 + j + q * 8 + it * 4
                            pool.wait_ge(blk_read, g + 1)
                            pool.wait_ge(h_ready, n + 2)
                            nc.gpsimd.tensor_tensor(relu2[:], relu[j % 2][:], relu[j % 2][:], ALU.mult)\
                                .then_inc(relu_squared, 1)
                            pool.wait_ge(relu_squared, n + 1)
                            pool.wait_ge(h_rounded, n + 1)
                            nc.gpsimd.tensor_tensor(h_lo[:, bass.ds(it * 4 + j, 1), :], chunk(relu2[:]),
                                                    h_hi[:, bass.ds(it * 4 + j, 1), :].bitcast(F32), ALU.subtract)\
                                .then_inc(h_ready, 1)

            add_squares(N_PRE_MIX0)
            pool.wait_ge(x_placed, NT + 1)
            pool.wait_ge(gain_placed, 1)
            pool.dma_start(tail_raw[:], mla_w_in[0].rearrange("(c p) m -> p c m", p=P)[:, :, 2 * LORA:])\
                .then_inc(tail_in, 16)
            pool.dma_start(uv[:], uv_v).then_inc(uv_in, 16)
            nc.gpsimd.memset(kT[0:NOPE, 0, :], 0.0).then_inc(k_zeroed, 1)
            for t in prob:
                nc.gpsimd.memset(t[:], 0.0)
            for t in probT:
                nc.gpsimd.memset(t[:], 0.0)
            nc.gpsimd.memset(v[:, 0, :], 0.0).then_inc(att_zeroed, 1)
            add_squares(N_CQ)
            add_squares(N_CKV)
            for i, (t0, n) in enumerate(TILES):
                pool.wait_ge(c_placed, i + 1)
                if i < NT:
                    pool.dma_start(new_ckv_prompt[0, 0, t0:t0 + n, :], ctok[0:n, i, 0:LORA]).then_inc(c_out, 16)
                    pool.dma_start(new_kpe_prompt[0, 0, t0:t0 + n, :], ctok[0:n, i, LORA:]).then_inc(c_out, 16)
                else:
                    pool.dma_start(new_ckv_sample[0].rearrange("b s c -> (b s) c"), ctok[0:n, i, 0:LORA]).then_inc(c_out, 16)
                    pool.dma_start(new_kpe_sample[0].rearrange("b s c -> (b s) c"), ctok[0:n, i, LORA:]).then_inc(c_out, 16)
            def load_head(h, s):
                pool.dma_start(wk_head[s][:], uk_v[:, :, bass.ds(h * NOPE, NOPE)]).then_inc(wk_in[s], 16)
                pool.dma_start(wq_head[s][:], uq_v[:, :, bass.ds(h * QH, QH)]).then_inc(wq_in[s], 16)

            def save_sample_queries(h, s):
                pool.wait_ge(q_roped, h * 2 + 2)
                nc.gpsimd.tensor_copy(qs[:, bass.ds(h, 1), :], chunk(qT[s][:, NP:T])).then_inc(qs_saved, 1)

            load_head(0, 0)
            load_head(1, 1)
            pool.dma_start(uk[:], uk_v).then_inc(uk_in, 16)
            with pool.Fori(0, HEADS // 2 - 1) as p:
                for s in range(2):
                    pool.wait_ge(piece_mm, p * (2 * PIECES) + PIECES * s + 4)
                    load_head(p * 2 + (s + 2), s)
                    save_sample_queries(p * 2 + s, s)
            for s in range(2):
                save_sample_queries(HEADS - 2 + s, s)
            pool.wait_ge(c_out, 16 * 2 * (NT + 1))
            boundary(N_POST_MIX0, 0, N_PRE_MLP0)
            nc.gpsimd.memset(y[:], 0.0).then_inc(y_zeroed, 1)
            mlp(0)
            boundary(N_POST_MLP0, 1, N_PRE_MIX1)
            x_wait(pool, 1, DC - 1)
            pool.dma_start(gd_raw[:], gla_w_in[0].rearrange("(c p) m -> p c m", p=P)[:, :, 3 * D:]).then_inc(gd_in, 16)
            pool.dma_start(wg[:], gla_w_gate[0]).then_inc(wg_in, 16)
            pool.wait_ge(gla_step, GLA_STEPS * GH)
            for b in range(NB + 1):
                if b < NB:
                    if b >= NST_S:
                        pool.wait_ge(st_out[b % NST_S], 16 * (b // NST_S))
                    pool.dma_start(sts[b % NST_S][:], state_gla[0, b].rearrange("h p v -> p h v")).then_inc(st_in[b % NST_S], 16)
                m = b - NST_S + 1
                if 0 <= m < NB:
                    pool.wait_ge(st_ready, m + 1)
                    pool.dma_start(new_gla_sample[0, m].rearrange("h p v -> p h v"), sts[m % NST_S][:])\
                        .then_inc(st_out[m % NST_S], 16)
            pool.wait_ge(state_ready, NCH)
            pool.dma_start(new_gla_prompt[0, 0].rearrange("h p v -> p h v"), stp[0][:]).then_inc(gp_out, 16)
            for h in range(GH):
                add_squares(N_GLA + h)
            for k in range(DC):
                pool.wait_ge(og_normed, k + 1)
                pool.wait_ge(silu_done, k + 1)
                nc.gpsimd.tensor_tensor(og[:, k, :], og[:, k, :], gr[:, k, :], ALU.mult).then_inc(og_gated, 1)
            for i in range(NST_S):
                pool.wait_ge(st_out[i], 16 * NB // NST_S)
            pool.wait_ge(gp_out, 16)
            boundary(N_POST_MIX1, 2, N_PRE_MLP1)
            nc.gpsimd.memset(y[:], 0.0).then_inc(y_zeroed, 1)
            mlp(1)
            boundary(N_POST_MLP1, 3)

        @block.scalar
        def _(act):
            def round_block(g, it=0):
                act.wait_ge(w_loaded[raw_slot(g)], it * 16 + 16 * (g // RAW + 1))
                if g >= SPLIT:
                    act.wait_ge(blk_mm, it * 4 + g - SPLIT + 1)
                nc.scalar.copy(w_hi[g % SPLIT][:], w_raw[raw_slot(g)][:]).then_inc(w_rounded, 1)

            def square(n, c, src):
                k = SQ0[n] + c
                if k >= 2:
                    act.wait_ge(sq_added, k - 1)
                nc.scalar.activation(sq[k % 2][:], src, ACT.Square).then_inc(squared, 1)

            def root(n):
                act.wait_ge(summed, n + 1)
                if n:
                    act.wait_ge(inverted, n)
                nc.scalar.activation(halves(std[:]), NORM_PS, ACT.Sqrt, bias=eps[:, 0:1], scale=1.0 / NORMS[n][1])\
                    .then_inc(rooted, 1)

            def round_x(c, row):
                nc.scalar.activation(act_hi[:, c, :], x[:, c, :], ACT.Identity, scale=gain[:, row + c:row + c + 1])\
                    .then_inc(act_rounded, 1)

            def norm_in(n, row, u):
                for c in range(DC):
                    x_wait(act, u, c)
                    round_x(c, row)
                    square(n, c, x[:, c, :])
                root(n)

            def square_y(n, it, j, g):
                k = SQ0[n] + j
                act.wait_ge(blk_read, it * 4 + g + j + 1)
                act.wait_ge(sq_added, it * 4 + k - 1)
                nc.scalar.activation(chunk(sq[j % 2][:]), y[:, bass.ds(it * 4 + j, 1), :], ACT.Square).then_inc(squared, 1)

            act.sem_inc(exp_done, 2)
            act.sem_inc(p_placed, 1)
            act.sem_inc(ss_exp, 1)
            act.sem_inc(sp_placed, 1)
            act.wait_ge(gain_placed, 1)
            act.wait_ge(x_placed, NT + 1)
            for c in range(DC):
                square(N_PRE_MIX0, c, x[:, c, :])
                round_x(c, R_PRE_MIX)
            round_block(0)
            round_block(1)
            root(N_PRE_MIX0)
            for g in range(4):
                round_block(g + 2)
            act.wait_ge(tail_in, 16)
            nc.scalar.copy(tail_hi[:], tail_raw[:]).then_inc(tail_rounded, 1)
            for n, c0 in ((N_CQ, 0), (N_CKV, LC)):
                for c in range(LC):
                    act.wait_ge(blk_read, c0 + c + 1)
                    square(n, c, lat[:, c0 + c, :])
                root(n)
            for i, (t0, n) in enumerate(TILES):
                act.wait_ge(c_turned, i + 1)
                nc.scalar.copy(ctok[0:n, i, :], ps[0:n, 4 + i % 2, 0:LORA + ROPE]).then_inc(c_placed, 1)
            act.wait_ge(att_zeroed, 1)
            for i, (t0, n) in enumerate(TILES[:NT]):
                act.wait_ge(v_mm, i + 1)
                nc.scalar.copy(v[0:n, i, :].rearrange("p (a n) -> p a n", a=2),
                               ps[0:n, 2 * (i % 2):2 * (i % 2) + 2, :]).then_inc(v_placed, 1)
            NST = 2 * NT
            def place_keys(h, s, a):
                act.wait_ge(piece_mm, h * PIECES + a + 1)
                nc.scalar.copy(kT[0:NOPE, s, NP // 2 * a:NP // 2 * (a + 1)], ps[0:NOPE, 6, 0:NP // 2]).then_inc(k_placed, 1)

            def head_pair(p, last=False):
                for n in range(NST + 2):
                    if n < NST:
                        rows = TILES[n % NT][1]
                        w = META + P * (n % NT)
                        act.wait_ge(bias_ready, p * NST + n + 1)
                        if n >= 3:
                            act.wait_ge(p_turned, p * NST + n - 2 + 2)
                        at = 1024 * (n % 2) + 512 - META
                        nc.scalar.activation(prob[n % 3][0:rows, 0:w], psf[0:rows, at:at + w], ACT.Exp,
                                             bias=stat[0:rows, 0, n:n + 1],
                                             accum_out=stat[0:rows, 1, n:n + 1]).then_inc(exp_done, 1)
                        if n % NT == 0 and not (last and n):
                            place_keys(p * 2 + (1 + n // NT), 1 - n // NT, 0)
                    if n >= 2:
                        m = n - 2
                        rows, nk = TILES[m % NT][1], m % NT
                        act.wait_ge(p_turned, p * NST + m + 1 + 2)
                        act.wait_ge(o_mm, p * NST + m - 1 + 2)
                        first = nc.scalar.copy(probT[m % 2][0:META, 0, 0:rows], psf[0:META, 2048:2048 + rows])
                        if nk == 0:
                            first.then_inc(p_placed, 1)
                        else:
                            first.then_inc(p_first, 1)
                            nc.scalar.copy(probT[m % 2][:, 1:1 + nk, 0:rows],
                                           psf[:, 2048 + P:2048 + P * (nk + 1)].rearrange("p (k n) -> p k n", n=P)[:, :, 0:rows])\
                                .then_inc(p_placed, 1)
                    if n % NT == 0 and n < NST and not (last and n):
                        place_keys(p * 2 + (1 + n // NT), 1 - n // NT, 1)

            place_keys(0, 0, 0)
            place_keys(0, 0, 1)
            with act.Fori(0, HEADS // 2 - 1) as p:
                head_pair(p)
            head_pair(HEADS // 2 - 1, last=True)
            for k in range(4):
                act.wait_ge(uk_turned, k + 1)
                nc.scalar.copy(ukT[:, 4 * k:4 * k + 4, :], psf[0:NOPE, 1024 * (k % 2):1024 * (k % 2) + 1024]
                               .rearrange("p (h c) -> p h c", h=4)).then_inc(uk_placed, 1)
            for i, (t0, n) in enumerate(TILES[:NT]):
                act.wait_ge(o_turned, i + 1)
                nc.scalar.copy(act_hi[:, :, t0:t0 + n], psf[:, 1024 * (i % 2):1024 * (i % 2) + 8 * n].rearrange("p (c n) -> p c n", c=DC))\
                    .then_inc(o_rounded, 1)

            def place_pages(b, k):
                act.wait_ge(pg_turned, b * 3 + k + 1)
                if k == 0:
                    act.wait_ge(ss_mm, b + 1)
                src = psf[:, 0:1024]
                if k == 0:
                    nc.scalar.copy(ckT[:, 0, :], src).then_inc(pg_placed, 1)
                else:
                    nc.scalar.copy(kpT[:], src[0:ROPE, :]).then_inc(pg_placed, 1)

            def sample_probs(b, last=False):
                act.wait_ge(ss_bias, b + 1)
                act.wait_ge(sp_turned, b + 1)
                nc.scalar.activation(sprob[0:HEADS * NS, :], psf[0:HEADS * NS, 2048:2048 + PAST + NSAM], ACT.Exp,
                                     bias=sstat[:, 0:1], accum_out=sstat[:, 1:2]).then_inc(ss_exp, 1)
                if not last:
                    place_pages(b + 1, 0)
                    place_pages(b + 1, 2)
                act.wait_ge(sp_turned, b + 1 + 1)
                act.wait_ge(so_mm, b + 3)
                nc.scalar.copy(sprobN[:], ps[0:NSAM, 6, P:P + HEADS * NS])
                nc.scalar.copy(sprobT[:], ps[:, 7, :].rearrange("p (k n) -> p k n", k=PAGES)).then_inc(sp_placed, 1)

            place_pages(0, 0)
            place_pages(0, 2)
            with act.Fori(0, NB - 1) as b:
                sample_probs(b)
            sample_probs(NB - 1, last=True)
            act.wait_ge(o_turned, NT + 1)
            nc.scalar.copy(act_hi[:, :, NP:T], ps[:, 0, 0:DC * NSAM].rearrange("p (c n) -> p c n", c=DC)).then_inc(o_rounded, 1)
            with act.Fori(0, 2) as it:
                for j in range(4):
                    round_block(G_MLA_O + j + 2, it)
                    square_y(N_POST_MIX0, it, j, G_MLA_O)

            def boundary(n_out, n_in, row, u):
                root(n_out)
                norm_in(n_in, row, u)

            def mlp_up(layer, q):
                g0 = G_MLP[layer]
                with act.Fori(0, 2) as it:
                    for j in range(4):
                        round_block(g0 + j + 2, q * 4 + it)
                        act.wait_ge(blk_read, g0 + j + 1 + q * 16 + it * 4)
                        nc.scalar.activation(h_hi[:, bass.ds(it * 4 + j, 1), :], chunk(relu[j % 2][:]),
                                             ACT.Square).then_inc(h_rounded, 1)

            def mlp_down(layer, q):
                with act.Fori(0, 2) as it:
                    for j in range(4):
                        round_block(G_MLP[layer] + 8 + j + 2, q * 4 + it)

            boundary(N_POST_MIX0, N_PRE_MLP0, R_PRE_MLP, 0)
            with act.Fori(0, 3) as q:
                mlp_up(0, q)
                mlp_down(0, q)
            mlp_up(0, 3)
            with act.Fori(0, 2) as it:
                for j in range(4):
                    round_block(G_MLP[0] + 56 + j + 2, it)
                    square_y(N_POST_MLP0, it, j, G_MLP[0] + 56)
            boundary(N_POST_MLP0, N_PRE_MIX1, R_PRE_MIX + 8, 1)
            with act.Fori(0, 4) as it:
                for j in range(4):
                    round_block(G_GLA_IN + j + 2, it)
            act.wait_ge(gd_in, 16)
            nc.scalar.copy(gd_hi[:], gd_raw[:]).then_inc(tail_rounded, 1)
            for j in range(8):
                round_block(G_GLA_IN + 16 + j + 2)
                h = j // 2
                if j % 2 == 0:
                    act.wait_ge(gate_mm, h + 1)
                    if h:
                        act.wait_ge(gla_step, GLA_STEPS * h)
                    nc.scalar.activation(halves(tA[:]), ps[:, 4:6, 0:HALF], ACT.Abs,
                                         bias=gain[:, R_BG + h:R_BG + h + 1]).then_inc(gla_act, 1)
                    act.wait_ge(gla_act, 6 * h + 1)
                    nc.scalar.activation(tA[:], tA[:], ACT.Exp, scale=-1.0).then_inc(gla_act, 1)
                    act.wait_ge(gla_act, 6 * h + 2)
                    nc.scalar.activation(tA[:], tA[:], ACT.Ln, bias=1.0).then_inc(gla_act, 1)
                else:
                    act.wait_ge(gla_step, GLA_STEPS * h + 3)
                    nc.scalar.activation(tB[:], bcum[:], ACT.Exp, scale=1.0 / TAU).then_inc(gla_act, 1)
                    nc.scalar.activation(tC[:], bcum[:], ACT.Exp, scale=-1.0 / TAU).then_inc(gla_act, 1)
                    act.wait_ge(gla_step, GLA_STEPS * h + 7)
                    nc.scalar.activation(tA[:], tA[:], ACT.Exp, scale=1.0 / TAU).then_inc(gla_act, 1)
            act.wait_ge(blk_read, G_GLA_IN + 24)
            for k in range(DC):
                nc.scalar.activation(gr[:, k, :], gr[:, k, :], ACT.Silu).then_inc(silu_done, 1)
            for i, (t0, n) in enumerate(TILES):
                act.wait_ge(kd_turned, i + 1)
                nc.scalar.copy(kd_tok[0:n, i, :], ps[0:n, 4 + i % 2, :]).then_inc(kd_placed, 1)
            for c in range(NCH):
                _, n, t0, _ = chunk_at(c)
                act.wait_ge(og_mm, c + 1)
                nc.scalar.copy(og[:, :, t0:t0 + n], ps[:, 5, :].rearrange("p (k n) -> p k n", k=DC)[:, :, 0:n])\
                    .then_inc(og_placed, 1)
            act.wait_ge(sup_mm, NB)
            nc.scalar.copy(og[:, :, NP:T], ps[:, 6, 0:DC * NSAM].rearrange("p (k n) -> p k n", k=DC)).then_inc(og_placed, 1)
            act.wait_ge(og_placed, NCH + 1)
            for h in range(GH):
                for c in range(2):
                    square(N_GLA + h, c, og[:, 2 * h + c, :])
                root(N_GLA + h)
            for k in range(DC):
                act.wait_ge(og_gated, k + 1)
                nc.scalar.copy(act_hi[:, k, :], og[:, k, :]).then_inc(act_rounded, 1)
            with act.Fori(0, 2) as it:
                for j in range(4):
                    round_block(G_GLA_O + j + 2, it)
                    square_y(N_POST_MIX1, it, j, G_GLA_O)
            boundary(N_POST_MIX1, N_PRE_MLP1, R_PRE_MLP + 8, 2)
            with act.Fori(0, 3) as q:
                mlp_up(1, q)
                mlp_down(1, q)
            mlp_up(1, 3)
            for j in range(8):
                if j < 6:
                    round_block(G_MLP[1] + 56 + j + 2)
                square_y(N_POST_MLP1, j // 4, j % 4, G_MLP[1] + 56)
            root(N_POST_MLP1)
            for i in (1, 3):
                act.wait_ge(y_turned, 1)
                nc.scalar.copy(out_tok[i][:], psf[:, 1024 * i:1024 * i + D]).then_inc(y_placed[1], 1)

        @block.vector
        def _(dve):
            def split_block(g, it=0):
                dve.wait_ge(w_rounded, it * 4 + g + 1)
                nc.vector.tensor_tensor(w_lo[g % SPLIT][:], w_raw[raw_slot(g)][:], w_hi[g % SPLIT][:].bitcast(F32),
                                        ALU.subtract).then_inc(w_split, 1)

            def invert(n, out):
                dve.wait_ge(rooted, n + 1)
                nc.vector.reciprocal(out[:], std[:]).then_inc(inverted, 1)

            def split_x(f, c, row):
                dve.wait_ge(act_rounded, 8 * f + c + 1)
                nc.vector.scalar_tensor_tensor(act_lo[:, c, :], x[:, c, :], gain[:, row + c:row + c + 1],
                                               act_hi[:, c, :].bitcast(F32), ALU.mult, ALU.subtract).then_inc(act_ready, 1)

            def boundary(n_out, row_out, u, n_in, f, row_in):
                invert(n_out, rstd_post)
                dve.wait_ge(inverted, n_out + 1)
                for c in range(DC):
                    nc.vector.scalar_tensor_tensor(y[:, c, :], y[:, c, :], gain[:, row_out + c:row_out + c + 1],
                                                   rstd_post[:], ALU.mult, ALU.mult).then_inc(y_normed, 1)
                    if c % 2 == 0 and c or c == DC - 1:
                        o = c - 1 if c % 2 == 0 else c
                        dve.wait_ge(y_normed, 8 * u + o + 1)
                        nc.vector.tensor_tensor(x[:, o, :], x[:, o, :], y[:, o, :], ALU.add).then_inc(x_updated[1], 1)
                    if c >= 2 and n_in is not None:
                        split_x(f, c - 2, row_in)
                if n_in is not None:
                    for c in range(DC - 2, DC):
                        split_x(f, c, row_in)
                    invert(n_in, rstd_pre)
                    dve.wait_ge(inverted, n_in + 1)

            dve.wait_ge(gain_turned, 1)
            nc.vector.tensor_copy(gain[:], ps[:, 4, 0:N_GAIN]).then_inc(gain_placed, 1)
            dve.sem_inc(o_placed, 2)
            dve.sem_inc(so_placed, 1)
            for i, (t0, n) in enumerate(TILES):
                dve.wait_ge(x_turned, i + 1)
                nc.vector.tensor_copy(x[:, :, t0:t0 + n], psf[:, 1024 * (i % 2):1024 * (i % 2) + DC * n]
                                      .rearrange("p (c n) -> p c n", c=DC)).then_inc(x_placed, 1)
            dve.wait_ge(gain_placed, 1)
            dve.wait_ge(x_placed, NT + 1)
            for c in range(DC):
                split_x(0, c, R_PRE_MIX)
            split_block(0)
            split_block(1)
            invert(N_PRE_MIX0, rstd_pre)
            dve.wait_ge(inverted, N_PRE_MIX0 + 1)
            for g in range(4):
                dve.wait_ge(blk_mm, g + 1)
                nc.vector.tensor_tensor(halves(lat[:, g, :]), blk_ps(g), halves(rstd_pre[:]), ALU.mult).then_inc(blk_read, 1)
                split_block(g + 2)
            dve.wait_ge(tail_rounded, 1)
            nc.vector.tensor_tensor(tail_lo[:], tail_raw[:], tail_hi[:].bitcast(F32), ALU.subtract).then_inc(tail_split, 1)
            kr = kT[NOPE:QH, 0, :]
            dve.wait_ge(tail_mm, 1)
            nc.vector.tensor_tensor(halves(kr), ps[0:ROPE, 4:6, 0:HALF], halves(rstd_pre[0:ROPE, :]), ALU.mult).then_inc(tail_read, 1)
            cos, sin = cst[NOPE:QH, C_COS:C_COS + T], cst[NOPE:QH, C_SIN:C_SIN + T]
            dve.wait_ge(krot_mm, 1)
            nc.vector.tensor_tensor(halves(rope_tmp[NOPE:QH, :]), ps[NOPE:QH, 4:6, 0:HALF], halves(sin), ALU.mult).then_inc(kpe_step, 1)
            nc.vector.tensor_tensor(kr, kr, cos, ALU.mult).then_inc(kpe_step, 1)
            dve.wait_ge(kpe_step, 2)
            nc.vector.tensor_tensor(kr, kr, rope_tmp[NOPE:QH, :], ALU.add).then_inc(kpe_step, 1)
            dve.wait_ge(kpe_step, 3)
            nc.vector.tensor_copy(kT[NOPE:QH, 1, :], kr).then_inc(kpe_ready, 1)
            for n, row, c0 in ((N_CQ, R_Q, 0), (N_CKV, R_KV, LC)):
                invert(n, rstd_post)
                dve.wait_ge(inverted, n + 1)
                for c in range(LC):
                    nc.vector.scalar_tensor_tensor(lat[:, c0 + c, :], lat[:, c0 + c, :], gain[:, row + c:row + c + 1],
                                                   rstd_post[:], ALU.mult, ALU.mult).then_inc(lat_ready, 1)
                dve.wait_ge(lat_ready, c0 + LC)
            NST = 2 * NT
            def place_queries(h, s, a):
                dve.wait_ge(piece_mm, h * PIECES + 2 + a + 1)
                dve.wait_ge(qs_saved, h + 1)
                nc.vector.tensor_scalar(qT[s][:, HALF * a:HALF * (a + 1)], ps[0:QH, 6, 0:HALF], SCALE, None, ALU.mult)\
                    .then_inc(q_placed, 1)

            def rotate_queries(h, s, a):
                cols = slice(HALF * a, HALF * (a + 1))
                qr = qT[s][NOPE:QH, cols]
                dve.wait_ge(piece_mm, h * PIECES + 4 + a + 1)
                nc.vector.tensor_tensor(rope_tmp[NOPE:QH, cols], ps[NOPE:QH, 6, 0:HALF], sin[:, cols], ALU.mult).then_inc(rope_step, 1)
                nc.vector.tensor_tensor(qr, qr, cos[:, cols], ALU.mult).then_inc(rope_step, 1)
                dve.wait_ge(rope_step, h * 4 + a * 2 + 2)
                nc.vector.tensor_tensor(qr, qr, rope_tmp[NOPE:QH, cols], ALU.add).then_inc(q_roped, 1)

            def head_pair(p, last=False):
                for n in range(NST + 3):
                    h, s = p * 2 + (1 + n // NT), 1 - n // NT
                    ahead = n < NST and not (last and n >= NT)
                    if n < NST:
                        rows = TILES[n % NT][1]
                        w = META + P * (n % NT)
                        at = 1024 * (n % 2) + 512 - META
                        dve.wait_ge(s_mm, p * NST + n + 1)
                        nc.vector.tensor_reduce(stat[0:rows, 0, n:n + 1], psf[0:rows, at:at + w], AX_X, ALU.max,
                                                negate=True).then_inc(bias_ready, 1)
                    if ahead and n % NT == 1:
                        place_queries(h, s, 0)
                    if ahead and n % NT == 2:
                        rotate_queries(h, s, 0)
                    if 1 <= n <= NST:
                        m = n - 1
                        rows = TILES[m % NT][1]
                        dve.wait_ge(exp_done, p * NST + m + 1 + 2)
                        nc.vector.reciprocal(stat[0:rows, 2, m:m + 1], stat[0:rows, 1, m:m + 1]).then_inc(rsum_inv, 1)
                    if n >= 3:
                        m = n - 3
                        rows = TILES[m % NT][1]
                        dve.wait_ge(o_mm, p * NST + m + 1 + 2)
                        dve.wait_ge(rsum_inv, p * NST + m + 1)
                        nc.vector.tensor_scalar(otok[0:rows, m % NT, bass.ds(p * (2 * VH) + (m // NT) * VH, VH)],
                                                ps[0:rows, 7, 0:VH], stat[0:rows, 2, m:m + 1], None, ALU.mult)\
                            .then_inc(o_placed, 1)
                    if ahead and n % NT == 1:
                        place_queries(h, s, 1)
                    if ahead and n % NT == 2:
                        rotate_queries(h, s, 1)

            for a in range(2):
                place_queries(0, 0, a)
            for a in range(2):
                rotate_queries(0, 0, a)
            with dve.Fori(0, HEADS // 2 - 1) as p:
                head_pair(p)
            head_pair(HEADS // 2 - 1, last=True)
            dve.wait_ge(qlat_mm, 1)
            for c in range(LC):
                nc.vector.tensor_copy(qlat[:, c, :, :].rearrange("p b (h s) -> p b h s", s=NS),
                                      ps[:, 4 + c, :].rearrange("p (h b s) -> p b h s", b=NB, s=NS)).then_inc(qlat_ready, 1)
            nc.vector.tensor_copy(qpe[:, :, :].rearrange("p b (h s) -> p b h s", s=NS),
                                  qs[NOPE:QH, :, :].rearrange("p h (b s) -> p b h s", s=NS)).then_inc(qlat_ready, 1)
            nc.vector.tensor_copy(kpe_new[:], kT[NOPE:QH, 0, NP:T]).then_inc(qlat_ready, 1)
            for i, (t0, n) in enumerate(TILES[:NT]):
                dve.wait_ge(o_rounded, i + 1)
                nc.vector.tensor_tensor(act_lo[:, :, t0:t0 + n], psf[:, 1024 * (i % 2):1024 * (i % 2) + 8 * n]
                                        .rearrange("p (c n) -> p c n", c=DC), act_hi[:, :, t0:t0 + n].bitcast(F32),
                                        ALU.subtract).then_inc(o_split, 1)
            dve.wait_ge(qlat_ready, 4)

            def take_queries(b):
                nc.vector.tensor_copy(qcur[:].rearrange("p c (o n) -> p c o n", o=1),
                                      qlat[:, :, bass.ds(b, 1), :])
                nc.vector.tensor_copy(chunk(qpcur[:]), qpe[:, bass.ds(b, 1), :]).then_inc(qcur_ready, 1)

            def place_pages(b):
                dve.wait_ge(pg_turned, b * 3 + 2)
                dve.wait_ge(ss_mm, b + 1)
                nc.vector.tensor_copy(ckT[:, 1, :], psf[:, 1024:2048])\
                    .then_inc(pg1_placed, 1)

            def take_output(b):
                dve.wait_ge(so_mm, b + 1 + 3)
                nc.vector.tensor_copy(olat[:, :, :, bass.ds(b * NS, NS)],
                                      ps[:, 7, 0:LC * HEADS * NS].rearrange("p (c h s) -> p c h s", c=LC, s=NS))\
                    .then_inc(so_placed, 1)

            def sample_stats(b, first=False, last=False):
                dve.wait_ge(ss_mm, b + 1 + 1)
                new = ps[0:HEADS * NS, 6, 0:NSAM]
                nc.vector.tensor_tensor(new, new, cst[0:HEADS * NS, bass.ds(b * NSAM + C_SMASK, NSAM)], ALU.add).then_inc(ss_step, 1)
                dve.wait_ge(ss_step, b * 2 + 1)
                nc.vector.tensor_reduce(sstat[:, 0:1], psf[0:HEADS * NS, 2048:2048 + PAST + NSAM], AX_X, ALU.max,
                                        negate=True).then_inc(ss_bias, 1)
                if not last:
                    take_queries(b + 1)
                if not first:
                    take_output(b - 1)
                dve.wait_ge(ss_exp, b + 1 + 1)
                nc.vector.reciprocal(sstat[:, 2:3], sstat[:, 1:2]).then_inc(ss_step, 1)
                dve.wait_ge(ss_step, b * 2 + 2)
                nc.vector.tensor_scalar(sprob[0:HEADS * NS, :], sprob[0:HEADS * NS, :], sstat[:, 2:3], None, ALU.mult).then_inc(ss_norm, 1)
                if not last:
                    place_pages(b + 1)

            nc.vector.memset(sprob[HEADS * NS:P, :], 0.0).then_inc(qcur_ready, 1)
            take_queries(0)
            place_pages(0)
            sample_stats(0, first=True)
            with dve.Fori(1, NB - 1) as b:
                sample_stats(b)
            sample_stats(NB - 1, last=True)
            take_output(NB - 1)
            dve.wait_ge(o_rounded, NT + 1)
            nc.vector.tensor_tensor(act_lo[:, :, NP:T], ps[:, 0, 0:DC * NSAM].rearrange("p (c n) -> p c n", c=DC),
                                    act_hi[:, :, NP:T].bitcast(F32), ALU.subtract).then_inc(o_split, 1)

            def product_to_y(g0):
                with dve.Fori(0, 2) as it:
                    for j in range(4):
                        dve.wait_ge(blk_mm, it * 4 + g0 + j + 1)
                        nc.vector.tensor_copy(y[:, bass.ds(it * 4 + j, 1), :].rearrange("p o (h n) -> p (o h) n", h=2),
                                              blk_ps(g0 + j)).then_inc(blk_read, 1)
                        split_block(g0 + j + 2, it)

            def mlp_up(layer, q):
                g0 = G_MLP[layer]
                with dve.Fori(0, 2) as it:
                    for j in range(4):
                        n = it * 4 + q * 8 + layer * 32 + j
                        dve.wait_ge(blk_mm, it * 4 + q * 16 + g0 + j + 1)
                        dve.wait_ge(h_ready, n + 1)
                        nc.vector.scalar_tensor_tensor(halves(relu[j % 2][:]), blk_ps(g0 + j), 0.0, halves(rstd_pre[:]),
                                                       ALU.max, ALU.mult).then_inc(blk_read, 1)
                        split_block(g0 + j + 2, q * 4 + it)

            def add_down(g, it, m, ahead=True):
                dve.wait_ge(blk_mm, it * 4 + g + 1)
                dve.wait_ge(blk_read, it * 4 + g)
                yc = y[:, bass.ds(m, 1), :].rearrange("p o (h n) -> p (o h) n", h=2)
                nc.vector.tensor_tensor(yc, blk_ps(g), yc, ALU.add).then_inc(blk_read, 1)
                if ahead:
                    split_block(g + 2, it)

            def mlp_down(layer, q):
                with dve.Fori(0, 2) as it:
                    for j in range(4):
                        add_down(G_MLP[layer] + 8 + j, q * 4 + it, it * 4 + j)

            dve.wait_ge(c_out, 16 * 2 * (NT + 1))
            product_to_y(G_MLA_O)
            boundary(N_POST_MIX0, R_POST_MIX, 0, N_PRE_MLP0, 1, R_PRE_MLP)
            dve.wait_ge(y_zeroed, 1)
            with dve.Fori(0, 4) as q:
                mlp_up(0, q)
                mlp_down(0, q)
            boundary(N_POST_MLP0, R_POST_MLP, 1, N_PRE_MIX1, 2, R_PRE_MIX + 8)
            with dve.Fori(0, 2) as it:
                for j in range(4):
                    dve.wait_ge(blk_mm, it * 4 + G_GLA_IN + j + 1)
                    nc.vector.tensor_tensor(gqk[:, bass.ds(it * 4 + j, 1), :].rearrange("p o (h n) -> p (o h) n", h=2),
                                            blk_ps(j), halves(rstd_pre[:]), ALU.mult).then_inc(blk_read, 1)
                    split_block(G_GLA_IN + j + 2, it)
            nc.vector.memset(gv[:, 0, :], 0.0).then_inc(att_cleared, 1)
            dve.wait_ge(att_cleared, 1)
            with dve.Fori(0, 2) as it:
                for j in range(4):
                    dve.wait_ge(blk_mm, it * 4 + G_GLA_IN + 8 + j + 1)
                    nc.vector.tensor_tensor(halves(vT[j][:]), blk_ps(j), halves(rstd_pre[:]), ALU.mult).then_inc(blk_read, 1)
                    split_block(G_GLA_IN + 8 + j + 2, it)
                for i, (t0, n) in enumerate(TILES):
                    dve.wait_ge(v_turned, it * (NT + 1) + i + 1)
                    nc.vector.tensor_copy(gv[0:n, i, bass.ds(it * 512, 512)], ps[0:n, 4 + i % 2, :]).then_inc(gv_placed, 1)
            dve.wait_ge(tail_rounded, 2)
            nc.vector.tensor_tensor(gd_lo[:], gd_raw[:], gd_hi[:].bitcast(F32), ALU.subtract).then_inc(tail_split, 1)
            dve.wait_ge(tail_mm, 2)
            nc.vector.tensor_tensor(halves(gdT[:]), ps[0:RANK, 4:6, 0:HALF], halves(rstd_pre[0:RANK, :]), ALU.mult)\
                .then_inc(gdT_ready, 1)
            step_count = 0

            def step(ins):
                nonlocal step_count
                step_count += 1
                ins.then_inc(gla_step, 1)
                dve.wait_ge(gla_step, step_count)

            def turns(ap, n):
                return ap.rearrange("p (k n) -> p k n", n=n)

            for j in range(8):
                dve.wait_ge(blk_mm, G_GLA_IN + 16 + j + 1)
                nc.vector.tensor_tensor(halves(gr[:, j, :]), blk_ps(j), halves(rstd_pre[:]), ALU.mult).then_inc(blk_read, 1)
                split_block(G_GLA_IN + 16 + j + 2)
                h = j // 2
                gq, gk = gqk[:, h, :], gqk[:, GH + h, :]
                if j % 2 == 0:
                    dve.wait_ge(gla_act, 6 * h + 1)
                    step(nc.vector.tensor_scalar(halves(tB[:]), ps[:, 4:6, 0:HALF], gain[:, R_BG + h:R_BG + h + 1], 0.0,
                                                 ALU.add, ALU.min))
                    dve.wait_ge(gla_act, 6 * h + 3)
                    step(nc.vector.tensor_tensor(tB[:], tB[:], tA[:], ALU.subtract))
                    step(nc.vector.tensor_tensor_scan(bcum[:], cst[:, C_SCAN:C_SCAN + T], tB[:], 0.0, ALU.mult, ALU.add))
                    continue
                dve.wait_ge(gla_act, 6 * h + 4)
                step(nc.vector.scalar_tensor_tensor(gq, gq, GSCALE, tB[:], ALU.mult, ALU.mult))
                spans = ((0, META, 1), (META, CH, SEQ // CH), (NP, NS, NB))
                for t0, n, k in spans:
                    b3 = turns(bcum[:, t0:t0 + n * k], n)
                    step(nc.vector.tensor_tensor(turns(tA[:, t0:t0 + n * k], n), b3[:, :, n - 1:n].to_broadcast([P, k, n]), b3,
                                                 ALU.subtract))
                dve.wait_ge(gla_act, 6 * h + 6)
                step(nc.vector.tensor_tensor(vT[h][:], gk, tA[:], ALU.mult))
                step(nc.vector.tensor_tensor(gk, gk, tC[:], ALU.mult))
                at = 0
                for t0, n, k in spans:
                    step(nc.vector.tensor_copy(chunk(decay[:, h, at:at + k]).rearrange("p o k -> p k o"),
                                               turns(tB[:, t0:t0 + n * k], n)[:, :, n - 1:n]))
                    at += k
            dve.wait_ge(tail_mm, 2)
            dve.wait_ge(kd_placed, 1)
            nc.vector.memset(attT[:], 0.0).then_inc(att_cleared, 1)
            dve.wait_ge(att_cleared, 2)
            dve.wait_ge(satt_mm, 1)
            nc.vector.tensor_tensor(attS[:], ps[0:NSAM, ATT_BANK[1], 0:GH * NSAM].rearrange("p (h n) -> p h n", h=GH),
                                    chunk(cst[0:NSAM, C_GSAM:C_GSAM + NSAM]).to_broadcast([NSAM, GH, NSAM]), ALU.mult)\
                .then_inc(satt_ready, 1)
            dve.wait_ge(kd_placed, NT + 1)

            def own_keys(b):
                if b >= 2:
                    dve.wait_ge(sup_mm, b - 1)
                nc.vector.tensor_scalar(kd_b[b % 2][:], kd_tok[0:NSAM, NT, :], cst[0:NSAM, C_GBM + b:C_GBM + b + 1], None,
                                        ALU.mult).then_inc(kdb_ready, 1)

            own_keys(0)
            own_keys(1)

            def sample_state(b):
                dve.wait_ge(sup_mm, b + 1)
                st = sts[b % NST_S]
                up = ps[:, 2:4, :].rearrange("p b (h v) -> p (b h) v", v=GV)
                for h in range(GH):
                    last = nc.vector.scalar_tensor_tensor(st[:, h, :], st[:, h, :], decay[:, h, NCH + b:NCH + b + 1], up[:, h, :],
                                                          ALU.mult, ALU.add)
                last.then_inc(st_ready, 1)
                if b + 2 < NB:
                    own_keys(b + 2)

            for c in range(NCH):
                base, n, t0, _ = chunk_at(c)
                dve.wait_ge(att_mm, c + 1)
                if c >= 2:
                    dve.wait_ge(og_mm, c - 1)
                rows = slice(base, base + n)
                nc.vector.tensor_tensor(attT[rows, att_slot(c), :, 0:n],
                                        ps[rows, ATT_BANK[c % 2], 0:GH * CH].rearrange("p (h n) -> p h n", h=GH)[:, :, 0:n],
                                        chunk(cst[rows, C_GTRI:C_GTRI + n]).to_broadcast([n, GH, n]), ALU.mult)\
                    .then_inc(att_ready, 1)
                dve.wait_ge(up_mm, c + 1)
                up = ps[:, 0:2, :].rearrange("p b (h v) -> p (b h) v", v=GV)
                if c == 0:
                    nc.vector.tensor_copy(stp[0][:], up).then_inc(state_ready, 1)
                else:
                    dve.wait_ge(og_mm, c)
                    dve.wait_ge(state_ready, c)
                    for h in range(GH):
                        last = nc.vector.scalar_tensor_tensor(stp[c % 2][:, h, :], stp[(c - 1) % 2][:, h, :], decay[:, h, c:c + 1],
                                                              up[:, h, :], ALU.mult, ALU.add)
                    last.then_inc(state_ready, 1)
                    sample_state(c - 1)
            for h in range(GH):
                invert(N_GLA + h, tmp[h])
                dve.wait_ge(inverted, N_GLA + h + 1)
                for c in range(2):
                    nc.vector.scalar_tensor_tensor(og[:, 2 * h + c, :], og[:, 2 * h + c, :], gain[:, R_GLA + c:R_GLA + c + 1],
                                                   tmp[h][:], ALU.mult, ALU.mult).then_inc(og_normed, 1)
            for k in range(DC):
                dve.wait_ge(act_rounded, 8 * 3 + k + 1)
                nc.vector.tensor_tensor(act_lo[:, k, :], og[:, k, :], act_hi[:, k, :].bitcast(F32), ALU.subtract)\
                    .then_inc(act_ready, 1)
            dve.wait_ge(gp_out, 16)
            for i in range(NST_S):
                dve.wait_ge(st_out[i], 16 * NB // NST_S)
            product_to_y(G_GLA_O)
            boundary(N_POST_MIX1, R_POST_MIX + 8, 2, N_PRE_MLP1, 4, R_PRE_MLP + 8)
            dve.wait_ge(y_zeroed, 2)
            with dve.Fori(0, 3) as q:
                mlp_up(1, q)
                mlp_down(1, q)
            mlp_up(1, 3)
            for j in range(8):
                add_down(G_MLP[1] + 3 * 16 + 8 + j, 0, j, ahead=j < 6)
            boundary(N_POST_MLP1, R_POST_MLP + 8, 3, None, None, None)
            for i in (0, 2, 4):
                n = TILES[i + 1][1]
                dve.wait_ge(y_turned, 1 + i // 4)
                nc.vector.tensor_copy(out_tok[i][0:n, :], psf[0:n, 1024 * (i % 4):1024 * (i % 4) + D]).then_inc(y_placed[0], 1)

        @block.tensor
        def _(pe):
            def block_product(g, it, ins_hi, ins_lo, ready=None):
                pe.wait_ge(w_split, it * 4 + g + 1)
                if g >= 2:
                    pe.wait_ge(blk_read, it * 4 + g - 1)
                out = ps[:, 2 * (g % 2):2 * (g % 2) + 2, :]
                for c in range(DC):
                    if ready is not None:
                        ready(c)
                    for k, (w, a) in enumerate(((w_hi, ins_hi), (w_hi, ins_lo), (w_lo, ins_hi))):
                        for h in range(2):
                            last = nc.tensor.matmul(out[:, h, 0:HALF], w[g % SPLIT][:, c, :], a[:, c, HALF * h:HALF * h + HALF],
                                                    start=(c == 0 and k == 0), stop=(c == DC - 1 and k == 2))
                last.then_inc(blk_mm, 1)

            def first_blocks(g, fill):
                for b in range(2):
                    pe.wait_ge(w_split, g + b + 1)
                    pe.wait_ge(blk_read, g + b - 1)
                for c in range(DC):
                    pe.wait_ge(act_ready, 8 * fill + c + 1)
                    for b in range(2):
                        for k, (w, a) in enumerate(((w_hi, act_hi), (w_hi, act_lo), (w_lo, act_hi))):
                            for h in range(2):
                                last = nc.tensor.matmul(ps[:, 2 * ((g + b) % 2) + h, 0:HALF], w[(g + b) % SPLIT][:, c, :],
                                                        a[:, c, HALF * h:HALF * h + HALF],
                                                        start=(c == 0 and k == 0), stop=(c == DC - 1 and k == 2))
                        if c == DC - 1:
                            last.then_inc(blk_mm, 1)

            def total(n):
                pe.wait_ge(sq_added, SQ0[n + 1])
                if n:
                    pe.wait_ge(rooted, n)
                for h in range(2):
                    last = nc.tensor.matmul(ps[:, 6 + h, 0:HALF], ones[:], ssum[:, HALF * h:HALF * h + HALF], start=True, stop=True)
                last.then_inc(summed, 1)

            def tail_product(w_a, w_b, m, n):
                pe.wait_ge(tail_split, n)
                for c in range(DC):
                    for k, (w, a) in enumerate(((w_a, act_hi), (w_a, act_lo), (w_b, act_hi))):
                        for h in range(2):
                            last = nc.tensor.matmul(ps[0:m, 4 + h, 0:HALF], w[:, c, :], a[:, c, HALF * h:HALF * h + HALF],
                                                    start=(c == 0 and k == 0), stop=(c == DC - 1 and k == 2))
                last.then_inc(tail_mm, 1)

            pe.sem_inc(p_turned, 2)
            pe.sem_inc(o_mm, 2)
            pe.sem_inc(ss_mm, 1)
            pe.sem_inc(sp_turned, 1)
            pe.sem_inc(so_mm, PG_S)
            pe.wait_ge(const_in, 16)
            pe.wait_ge(gain_in, 16 * 8)
            nc.tensor.transpose(ps[:, 4, 0:N_GAIN], gain_rows[:], ident[0:N_GAIN, 0:N_GAIN]).then_inc(gain_turned, 1)
            for i, (t0, n) in enumerate(TILES):
                if i in (0, 1, NT):
                    pe.wait_ge(x_in[(0, 1, NT).index(i)], 16)
                if i >= 2:
                    pe.wait_ge(x_placed, i - 1)
                for c in range(DC):
                    at = 1024 * (i % 2) + n * c
                    last = nc.tensor.transpose(psf[:, at:at + n], x_tok[0:n, i, P * c:P * c + P], ident[0:n, 0:n])
                last.then_inc(x_turned, 1)
            pe.wait_ge(ones_set, 1)
            pe.wait_ge(x_placed, NT + 1)
            total(N_PRE_MIX0)
            for g in range(4):
                block_product(g, 0, act_hi, act_lo, ready=(lambda c: pe.wait_ge(act_ready, c + 1)) if g == 0 else None)
            tail_product(tail_hi, tail_lo, ROPE, 1)
            rot = cst[0:QH, C_ROT:C_ROT + QH]
            pe.wait_ge(tail_read, 1)
            pe.wait_ge(k_zeroed, 1)
            for h in range(2):
                last = nc.tensor.matmul(ps[0:QH, 4 + h, 0:HALF], rot, kT[:, 0, HALF * h:HALF * h + HALF], start=True, stop=True)
            last.then_inc(krot_mm, 1)
            total(N_CQ)
            total(N_CKV)
            pe.wait_ge(lat_ready, 2 * LC)
            pe.wait_ge(kpe_ready, 1)
            for i, (t0, n) in enumerate(TILES):
                if i >= 2:
                    pe.wait_ge(c_placed, i - 1)
                for c in range(LC):
                    nc.tensor.transpose(ps[0:n, 4 + i % 2, P * c:P * c + P], lat[:, LC + c, t0:t0 + n], ident)
                nc.tensor.transpose(ps[0:n, 4 + i % 2, LORA:LORA + ROPE], kT[NOPE:QH, 0, t0:t0 + n],
                                    ident[NOPE:QH, NOPE:QH]).then_inc(c_turned, 1)
            pe.wait_ge(uv_in, 16)
            pe.wait_ge(blk_read, 4)
            for i, (t0, n) in enumerate(TILES[:NT]):
                if i >= 2:
                    pe.wait_ge(v_placed, i - 1)
                for a in range(2):
                    for c in range(LC):
                        last = nc.tensor.matmul(ps[0:n, 2 * (i % 2) + a, :], lat[:, LC + c, t0:t0 + n], uv[:, c, 512 * a:512 * a + 512],
                                                start=(c == 0), stop=(c == LC - 1))
                last.then_inc(v_mm, 1)
            pe.wait_ge(v_placed, NT)
            pe.wait_ge(c_placed, NT + 1)
            NST = 2 * NT

            def head_scores(p, n):
                hh, i = n // NT, n % NT
                t0, rows = TILES[i]
                pe.wait_ge(exp_done, p * NST + n - 2 + 1 + 2)
                rows = P
                q = qT[hh][:, t0:t0 + rows]
                at = 1024 * (n % 2) + 512
                nc.tensor.matmul(psf[0:rows, at - META:at], q, kT[:, hh, 0:META], start=True, stop=(i > 0))
                if i:
                    nc.tensor.matmul(psf[0:rows, at:at + P * i], q, kT[:, hh, META:META + P * i], start=True, stop=False)
                w = TILES[i][1]
                d = at + P * (i - 1) if i else at - META
                last = nc.tensor.matmul(psf[0:rows, d:d + w], ident, cst[:, C_TRI:C_TRI + w], start=False, stop=True)
                last.then_inc(s_mm, 1)

            def turn_probs(p, n):
                i = n % NT
                pe.wait_ge(exp_done, p * NST + n + 1 + 2)
                pe.wait_ge(p_placed, p * NST + n + 1)
                for k in range(i, -1, -1):
                    t0, nk = TILES[k] if i else (0, P)
                    last = nc.tensor.transpose(psf[0:nk, 2048 + P * k:2048 + P * k + P], prob[n % 3][:, t0:t0 + nk], ident)
                last.then_inc(p_turned, 1)

            def head_out(p, n):
                hh, i = n // NT, n % NT
                pe.wait_ge(p_placed, p * NST + n + 1 + 1)
                pe.wait_ge(o_placed, p * NST + n + 2)
                for k in range(i + 1):
                    last = nc.tensor.matmul(ps[:, 7, 0:VH], probT[n % 2][:, k, :],
                                            v[:, k, bass.ds(p * (2 * VH) + hh * VH, VH)], start=(k == 0), stop=(k == i))
                last.then_inc(o_mm, 1)

            def piece(h, s, turn, k):
                a = k % 2
                if k == 0:
                    pe.wait_ge(wk_in[s], turn * 16 + 16)
                    if not isinstance(h, int):
                        pe.wait_ge(q_roped, h * 2)
                elif k <= 2:
                    pe.wait_ge(k_placed, h * 2 + k)
                    if k == 2:
                        pe.wait_ge(wq_in[s], turn * 16 + 16)
                elif k <= 4:
                    pe.wait_ge(q_placed, h * 2 + k - 2)
                else:
                    pe.wait_ge(q_roped, h * 2 + 1)
                if k < 2:
                    for c in range(LC):
                        last = nc.tensor.matmul(ps[0:NOPE, 6, 0:NP // 2], wk_head[s][:, c, :],
                                                lat[:, LC + c, NP // 2 * a:NP // 2 * (a + 1)], start=(c == 0), stop=(c == LC - 1))
                elif k < 4:
                    for c in range(LC):
                        last = nc.tensor.matmul(ps[0:QH, 6, 0:HALF], wq_head[s][:, c, :], lat[:, c, HALF * a:HALF * (a + 1)],
                                                start=(c == 0), stop=(c == LC - 1))
                else:
                    last = nc.tensor.matmul(ps[0:QH, 6, 0:HALF], rot, qT[s][:, HALF * a:HALF * (a + 1)], start=True, stop=True)
                last.then_inc(piece_mm, 1)

            def head_pair(p, last=False):
                for n in range(NST + 3):
                    i = n % NT
                    h, s = p * 2 + (1 + n // NT), 1 - n // NT
                    ahead = n < NST and i < 3 and not (last and n >= NT)
                    if n < NST:
                        if i == 0:
                            pe.wait_ge(k_placed, p * 4 + n // NT * 2 + 2)
                            pe.wait_ge(q_roped, p * 4 + n // NT * 2 + 2)
                        head_scores(p, n)
                    if ahead:
                        piece(h, s, p + n // NT, 2 * i)
                    if 2 <= n < NST + 2:
                        turn_probs(p, n - 2)
                    if ahead:
                        piece(h, s, p + n // NT, 2 * i + 1)
                    if n >= 3:
                        head_out(p, n - 3)

            for k in range(PIECES):
                piece(0, 0, 0, k)
            with pe.Fori(0, HEADS // 2 - 1) as p:
                head_pair(p)
            head_pair(HEADS // 2 - 1, last=True)
            pe.wait_ge(uk_in, 16)
            pe.wait_ge(o_placed, HEADS * NT + 2)
            for k in range(4):
                if k >= 2:
                    pe.wait_ge(uk_placed, k - 1)
                for hh in range(4):
                    for c in range(LC):
                        at = 1024 * (k % 2) + LORA * hh + P * c
                        last = nc.tensor.transpose(psf[0:NOPE, at:at + P], uk[:, c, NOPE * (4 * k + hh):NOPE * (4 * k + hh + 1)], ident)
                last.then_inc(uk_turned, 1)
            pe.wait_ge(uk_placed, 4)
            pe.wait_ge(qs_saved, HEADS + 2)
            for h in range(HEADS):
                for c in range(LC):
                    last = nc.tensor.matmul(ps[:, 4 + c, NSAM * h:NSAM * h + NSAM], ukT[:, h, P * c:P * c + P], qs[0:NOPE, h, :],
                                            start=True, stop=True)
            last.then_inc(qlat_mm, 1)
            for i, (t0, n) in enumerate(TILES[:NT]):
                if i >= 2:
                    pe.wait_ge(o_split, i - 1)
                for c in range(DC):
                    at = 1024 * (i % 2) + n * c
                    last = nc.tensor.transpose(psf[:, at:at + n], otok[0:n, i, P * c:P * c + P], ident[0:n, 0:n])
                last.then_inc(o_turned, 1)

            def turn_pages(b, s, turn):
                pe.wait_ge(page_in[s], turn * (2 * PAGES * 16) + 2 * PAGES * 16)
                for k in range(3):
                    if k == 2:
                        pe.wait_ge(pg_placed, b * 2 + 1)
                    for g in range(PAGES):
                        at = 1024 * (k % 2) + P * g
                        if k < LC:
                            last = nc.tensor.transpose(psf[:, at:at + P], pg_ckv[s][:, g, P * k:P * k + P], ident)
                        else:
                            last = nc.tensor.transpose(psf[0:ROPE, at:at + P], pg_kpe[s][:, g, :], ident)
                    last.then_inc(pg_turned, 1)

            rows = HEADS * NS

            def sample_scores(b):
                pe.wait_ge(qcur_ready, b + 2)
                pe.wait_ge(pg_placed, b * 2 + 2)
                pe.wait_ge(pg1_placed, b + 1)
                pe.wait_ge(ss_exp, b + 1)
                for a in range(2):
                    for c in range(LC):
                        nc.tensor.matmul(ps[0:rows, 4 + a, :], qcur[:, c, :], ckT[:, c, 512 * a:512 * a + 512],
                                         start=(c == 0), stop=False)
                    nc.tensor.matmul(ps[0:rows, 4 + a, :], qpcur[:], kpT[:, 512 * a:512 * a + 512], start=False, stop=True)
                pe.wait_ge(sp_placed, b + 1)
                for c in range(LC):
                    nc.tensor.matmul(ps[0:rows, 6, 0:NSAM], qcur[:, c, :], lat[:, LC + c, NP:T], start=(c == 0), stop=False)
                nc.tensor.matmul(ps[0:rows, 6, 0:NSAM], qpcur[:], kpe_new[:], start=False, stop=True).then_inc(ss_mm, 1)

            def turn_sample_probs(b):
                pe.wait_ge(ss_norm, b + 1)
                pe.wait_ge(so_placed, b + 1)
                nc.tensor.transpose(ps[:, 7, 0:P], sprob[:, 0:P], ident)
                for g in range(1, PAGES):
                    nc.tensor.transpose(ps[:, 7, rows * g:rows * g + rows], sprob[0:rows, P * g:P * g + P], ident[0:rows, 0:rows])
                last = nc.tensor.transpose(ps[0:NSAM, 6, P:P + rows], sprob[0:rows, PAST:PAST + NSAM], ident[0:rows, 0:rows])
                last.then_inc(sp_turned, 1)

            def sample_out(b, s):
                pe.wait_ge(sp_placed, b + 1 + 1)
                for c in range(LC):
                    out = ps[:, 7, rows * c:rows * (c + 1)]
                    for g in range(PAGES):
                        nc.tensor.matmul(out, pg_ckv[s][:, g, P * c:P * c + P], sprobT[:, g, :], start=(g == 0), stop=False)
                    last = nc.tensor.matmul(out, ctok[0:NSAM, NT, P * c:P * c + P], sprobN[:], start=False, stop=True)
                last.then_inc(so_mm, 1)

            def sample_attention(b, s, turn, last_one=False):
                sample_scores(b)
                sample_out(b - 1, (s - 2) % PG_S)
                if not last_one:
                    turn_pages(b + 1, s, turn)
                turn_sample_probs(b)

            pe.wait_ge(qlat_ready, 4)
            pe.wait_ge(o_split, NT)
            turn_pages(0, 0, 0)
            sample_scores(0)
            turn_pages(1, 1, 0)
            turn_sample_probs(0)
            with pe.Fori(0, (NB - 2) // PG_S) as i:
                for s in range(PG_S):
                    sample_attention(i * PG_S + (s + 1), (s + 2) % PG_S, i + (s + 2) // PG_S)
            for b in range((NB - 2) // PG_S * PG_S + 1, NB):
                sample_attention(b, (b + 1) % PG_S, (b + 1) // PG_S, last_one=(b == NB - 1))
            sample_out(NB - 1, (NB - 1) % PG_S)
            pe.wait_ge(so_placed, NB + 1)
            for h in range(HEADS):
                for c in range(LC):
                    last = nc.tensor.matmul(ps[VH * (h % 2):VH * (h % 2) + VH, 0, NSAM * (h // 2):NSAM * (h // 2) + NSAM],
                                            uv[:, c, VH * h:VH * h + VH], olat[:, c, h, :], start=(c == 0), stop=(c == LC - 1))
            last.then_inc(o_turned, 1)
            pe.wait_ge(o_split, NT + 1)
            with pe.Fori(0, 2) as it:
                for j in range(4):
                    block_product(G_MLA_O + j, it, act_hi, act_lo)

            def mlp_up(layer, q):
                with pe.Fori(0, 2) as it:
                    for j in range(4):
                        block_product(G_MLP[layer] + j, q * 4 + it, act_hi, act_lo)

            def mlp_down(layer, q):
                with pe.Fori(0, 2) as it:
                    for j in range(4):
                        block_product(G_MLP[layer] + 8 + j, q * 4 + it, h_hi, h_lo,
                                      ready=(lambda c: pe.wait_ge(h_ready, q * 8 + layer * 32 + c + 1 + 2)) if j == 0 else None)

            def boundary(n_out, n_in, fill, g):
                total(n_out)
                first_blocks(g, fill)
                total(n_in)
                for j in range(2, 4):
                    block_product(g + j, 0, act_hi, act_lo)

            def mlp(layer):
                for j in range(4):
                    block_product(G_MLP[layer] + j, 1, act_hi, act_lo)
                mlp_down(layer, 0)
                with pe.Fori(1, 4) as q:
                    mlp_up(layer, q)
                    mlp_down(layer, q)

            boundary(N_POST_MIX0, N_PRE_MLP0, 1, G_MLP[0])
            mlp(0)
            boundary(N_POST_MLP0, N_PRE_MIX1, 2, G_GLA_IN)
            for j in range(4):
                block_product(G_GLA_IN + j, 1, act_hi, act_lo)
            with pe.Fori(0, 2) as it:
                for j in range(4):
                    block_product(G_GLA_IN + 8 + j, it, act_hi, act_lo)
                pe.wait_ge(blk_read, it * 4 + G_GLA_IN + 8 + 4)
                for i, (t0, n) in enumerate(TILES):
                    if i >= 2:
                        pe.wait_ge(gv_placed, it * (NT + 1) + i - 1)
                    for j in range(4):
                        last = nc.tensor.transpose(ps[0:n, 4 + i % 2, P * j:P * j + P], vT[j][:, t0:t0 + n], ident)
                    last.then_inc(v_turned, 1)
            pe.wait_ge(gv_placed, 2 * (NT + 1))
            tail_product(gd_hi, gd_lo, RANK, 2)
            pe.wait_ge(gdT_ready, 1)
            pe.wait_ge(wg_in, 16)
            for j in range(8):
                h = j // 2
                if j % 2 == 0:
                    if h:
                        pe.wait_ge(gla_step, GLA_STEPS * (h - 1) + 1)
                    for a in range(2):
                        last = nc.tensor.matmul(ps[:, 4 + a, 0:HALF], wg[:, GK * h:GK * h + GK],
                                                gdT[:, HALF * a:HALF * a + HALF], start=True, stop=True)
                    last.then_inc(gate_mm, 1)
                block_product(G_GLA_IN + 16 + j, 0, act_hi, act_lo)
            pe.wait_ge(gla_step, GLA_STEPS * GH)
            for i, (t0, n) in enumerate(TILES):
                if i >= 2:
                    pe.wait_ge(kd_placed, i - 1)
                for h in range(GH):
                    last = nc.tensor.transpose(ps[0:n, 4 + i % 2, GK * h:GK * h + GK], vT[h][:, t0:t0 + n], ident)
                last.then_inc(kd_turned, 1)
            pe.wait_ge(kd_placed, NT + 1)
            pe.wait_ge(blk_read, G_GLA_IN + 24)

            def chunk_out(c):
                base, n, t0, tile = chunk_at(c)
                pe.wait_ge(att_ready, c + 1)
                if c:
                    pe.wait_ge(state_ready, c)
                    pe.wait_ge(og_placed, c)
                for k in range(2 * GH):
                    h, a = k // 2, k % 2
                    out = ps[:, 5, CH * k:CH * k + n]
                    last = nc.tensor.matmul(out, gv[:, tile, P * k:P * k + P], attT[:, att_slot(c), h, 0:n], start=True, stop=(c == 0))
                    if c:
                        last = nc.tensor.matmul(out, stp[(c - 1) % 2][:, h, P * a:P * a + P], gqk[:, h, t0:t0 + n],
                                                start=False, stop=True)
                last.then_inc(og_mm, 1)

            for h in range(GH):
                last = nc.tensor.matmul(ps[0:NSAM, ATT_BANK[1], NSAM * h:NSAM * h + NSAM], gqk[:, GH + h, NP:T], gqk[:, h, NP:T],
                                        start=True, stop=True)
            last.then_inc(satt_mm, 1)
            pe.wait_ge(satt_ready, 1)
            for k in range(2 * GH):
                nc.tensor.matmul(ps[:, 6, NSAM * k:NSAM * k + NSAM], gv[0:NSAM, NT, P * k:P * k + P], attS[:, k // 2, :],
                                 start=(k == 0), stop=False, skip_group_check=True)

            def sample_batch(b):
                pe.wait_ge(st_in[b % NST_S], 16 * (b // NST_S + 1))
                for k in range(2 * GH):
                    at = NSAM * k + NS * b
                    nc.tensor.matmul(ps[:, 6, at:at + NS], sts[b % NST_S][:, k // 2, P * (k % 2):P * (k % 2) + P],
                                     gqk[:, k // 2, NP + NS * b:NP + NS * b + NS], start=False, stop=(b == NB - 1),
                                     skip_group_check=True)
                pe.wait_ge(kdb_ready, b + 1)
                if b:
                    pe.wait_ge(st_ready, b)
                for h in range(GH):
                    last = nc.tensor.matmul(ps[:, 2 + h // 2, GV * (h % 2):GV * (h % 2) + GV],
                                            kd_b[b % 2][:, GK * h:GK * h + GK], gv[0:NSAM, NT, GV * h:GV * h + GV],
                                            start=True, stop=True)
                last.then_inc(sup_mm, 1)

            for c in range(NCH):
                base, n, t0, tile = chunk_at(c)
                if c >= 2:
                    pe.wait_ge(att_ready, c - 1)
                elif c:
                    pe.wait_ge(satt_ready, 1)
                for h in range(GH):
                    last = nc.tensor.matmul(ps[base:base + n, ATT_BANK[c % 2], CH * h:CH * h + n], gqk[:, GH + h, t0:t0 + n],
                                            gqk[:, h, t0:t0 + n], start=True, stop=True)
                last.then_inc(att_mm, 1)
                if c >= 1:
                    pe.wait_ge(state_ready, c)
                for h in range(GH):
                    last = nc.tensor.matmul(ps[:, h // 2, GV * (h % 2):GV * (h % 2) + GV],
                                            kd_tok[base:base + n, tile, GK * h:GK * h + GK],
                                            gv[base:base + n, tile, GV * h:GV * h + GV], start=True, stop=True)
                last.then_inc(up_mm, 1)
                if c >= 1:
                    chunk_out(c - 1)
                    sample_batch(c - 1)
            chunk_out(NCH - 1)
            pe.wait_ge(og_placed, NCH + 1)
            for h in range(GH):
                total(N_GLA + h)
            pe.wait_ge(act_ready, 8 * 4)
            pe.wait_ge(st_ready, NB)
            with pe.Fori(0, 2) as it:
                for j in range(4):
                    block_product(G_GLA_O + j, it, act_hi, act_lo)
            boundary(N_POST_MIX1, N_PRE_MLP1, 4, G_MLP[1])
            mlp(1)
            total(N_POST_MLP1)
            pe.wait_ge(rooted, len(NORMS))
            pe.wait_ge(blk_read, G_END)
            for c in range(DC):
                x_wait(pe, 3, c)
                for i, (t0, n) in enumerate(TILES[1:NT]):
                    at = 1024 * i + P * c
                    last = nc.tensor.transpose(psf[0:n, at:at + P], x[:, c, t0:t0 + n], ident)
            last.then_inc(y_turned, 1)
            pe.wait_ge(y_placed[0], 1)
            t0, n = TILES[NT]
            for c in range(DC):
                last = nc.tensor.transpose(psf[0:n, P * c:P * c + P], x[:, c, t0:t0 + n], ident)
            last.then_inc(y_turned, 1)


_INS = ['x_prompt', 'x_sample', 'cache_ckv', 'cache_kpe', 'state_gla', 'page_table', 'meta_tokens', 'norm_pre_mix',
        'norm_post_mix', 'norm_pre_mlp', 'norm_post_mlp', 'mla_w_in', 'mla_q_norm', 'mla_w_uq', 'mla_kv_norm',
        'mla_w_uk', 'mla_w_uv', 'mla_w_o', 'gla_w_in', 'gla_w_gate', 'gla_b_gate', 'gla_norm', 'gla_w_o',
        'mlp_w_up', 'mlp_w_down']
_OUTS = [(1, SEQ, D), (NB, NS, D), (1, 1, NP, LORA), (1, 1, NP, ROPE), (1, NB, NS, LORA), (1, NB, NS, ROPE),
         (1, 1, GH, GK, GV), (1, NB, GH, GK, GV)]


def kernel(**inputs):
    import numpy as _np
    import concourse.bacc as _bacc
    from concourse import mybir as _mybir
    from concourse.bass_utils import run_bass_kernel_spmd as _run

    nc = _bacc.Bacc("TRN2", target_bir_lowering=False, num_devices=1)
    arrays, args = {}, []
    for name in _INS:
        a = _np.ascontiguousarray(inputs[name])
        arrays[f"in_{name}_dram"] = a
        args.append(nc.dram_tensor(f"in_{name}_dram", a.shape, _mybir.dt.from_np(a.dtype), kind="ExternalInput").ap())
    arrays["const_dram"] = constants()
    args.append(nc.dram_tensor("const_dram", (P, N_CONST), _mybir.dt.float32, kind="ExternalInput").ap())
    for i, shape in enumerate(_OUTS):
        args.append(nc.dram_tensor(f"out_{i}_dram", shape, _mybir.dt.float32, kind="ExternalOutput").ap())
    trunk(nc, *args)
    r = _run(nc, [arrays], core_ids=[0])
    return tuple(r.results[0][f"out_{i}_dram"] for i in range(len(_OUTS)))
```
